# Optimizing a Trainium2 kernel written in Bass

```python
import jax, jax.numpy as jnp
from jax import lax
import numpy as np

D_MODEL = 1024
BATCH = 1
SEQ = 512
DEPTH = 2

CHUNK = 64
N_META = 16
BLOCK_Q = 128
EPS = 1e-6

SB_HEADS = 8
SB_HEAD_DIM = D_MODEL // 16
SB_WIDTH = SB_HEADS * SB_HEAD_DIM
CONV_CH = D_MODEL // 2
CONV_K = 3
IN_COLS = 3 * SB_WIDTH + 3 * CONV_CH

POOL_WINDOWS = (2, 4, 8, 16)
POOL_CH = D_MODEL // len(POOL_WINDOWS)

PEER_HEADS = 8
PEER_NKEYS = 128
PEER_N = PEER_NKEYS * PEER_NKEYS
PEER_TOPK = 16
PEER_HALF = 128
PEER_TOKEN_BLOCK = 128

N_EVEN = (DEPTH + 1) // 2
N_ODD = DEPTH // 2

kernel_name = 'hybrid_stickbreak_conv_pool_peer_encoder'

def rms_norm(x, g):
    xf = x.astype(jnp.float32)
    y = xf * lax.rsqrt(jnp.mean(xf * xf, axis=-1, keepdims=True) + EPS)
    return (y * g.astype(jnp.float32)).astype(x.dtype)

def stick_breaking_attention(q, k, v):
    b, h, lp, dh = q.shape
    nb = lp // BLOCK_Q
    scale = dh ** -0.5
    kf = k.astype(jnp.float32)
    vf = v.astype(jnp.float32)
    qb = q.astype(jnp.float32).reshape(b, h, nb, BLOCK_Q, dh).transpose(2, 0, 1, 3, 4)
    key_pos = jnp.arange(lp)

    def one_block(args):
        q_blk, blk = args
        z = jnp.einsum('bhqd,bhkd->bhqk', q_blk, kf) * scale
        q_pos = blk * BLOCK_Q + jnp.arange(BLOCK_Q)
        causal = key_pos[None, :] < q_pos[:, None]
        log_keep = jnp.where(causal, jax.nn.log_sigmoid(-z), 0.0)
        later = lax.cumsum(log_keep, axis=3, reverse=True) - log_keep
        w = jnp.where(causal, jnp.exp(jax.nn.log_sigmoid(z) + later), 0.0)
        return jnp.einsum('bhqk,bhkd->bhqd', w, vf)

    out = lax.map(one_block, (qb, jnp.arange(nb)))
    return out.transpose(1, 2, 0, 3, 4).reshape(b, h, lp, dh).astype(v.dtype)

def causal_short_conv(u, w):
    lp = u.shape[1]
    up = jnp.pad(u, ((0, 0), (CONV_K - 1, 0), (0, 0)))
    y = w[0] * up[:, 0:lp]
    for i in range(1, CONV_K):
        y = y + w[i] * up[:, i:i + lp]
    return y

def even_layer(x, norm_g, w_in, q_g, k_g, conv_w, w_out):
    b, lp, _ = x.shape
    h = rms_norm(x, norm_g)
    proj = h @ w_in
    cuts = [SB_WIDTH, 2 * SB_WIDTH, 3 * SB_WIDTH, 3 * SB_WIDTH + CONV_CH, 3 * SB_WIDTH + 2 * CONV_CH]
    q, k, v, gate_b, gate_c, u = jnp.split(proj, cuts, axis=-1)
    q = rms_norm(q.reshape(b, lp, SB_HEADS, SB_HEAD_DIM), q_g).transpose(0, 2, 1, 3)
    k = rms_norm(k.reshape(b, lp, SB_HEADS, SB_HEAD_DIM), k_g).transpose(0, 2, 1, 3)
    v = v.reshape(b, lp, SB_HEADS, SB_HEAD_DIM).transpose(0, 2, 1, 3)
    att = stick_breaking_attention(q, k, v).transpose(0, 2, 1, 3).reshape(b, lp, SB_WIDTH)
    conv = gate_b * causal_short_conv(gate_c * u, conv_w)
    return jnp.concatenate([att, conv], axis=-1) @ w_out

def odd_layer(x, norm_g, pool_w, pool_scale):
    b, lp, _ = x.shape
    hf = rms_norm(x, norm_g).astype(jnp.float32)
    csum = jnp.pad(jnp.cumsum(hf, axis=1), ((0, 0), (1, 0), (0, 0)))
    count = jnp.arange(1, lp + 1).astype(jnp.float32)
    diffs = []
    for g, w in enumerate(POOL_WINDOWS):
        sl = slice(g * POOL_CH, (g + 1) * POOL_CH)
        c = csum[:, :, sl]
        lo = jnp.pad(c, ((0, 0), (w - 1, 0), (0, 0)))[:, :lp]
        mean = (c[:, 1:] - lo) / jnp.minimum(count, float(w))[None, :, None]
        diffs.append(mean - hf[:, :, sl])
    d = jnp.stack(diffs, axis=2)
    y = jnp.einsum('blgc,gce->blge', d, pool_w.astype(jnp.float32)).reshape(b, lp, D_MODEL)
    return (y * pool_scale.astype(jnp.float32)).astype(x.dtype)

def peer_ffn(x, norm_g, w_query, sub_keys, expert_u, expert_v):
    b, lp, d = x.shape
    h = rms_norm(x, norm_g).reshape(-1, PEER_TOKEN_BLOCK, d)
    keys = sub_keys.astype(jnp.float32)

    def one_block(hb):
        t = hb.shape[0]
        q = (hb @ w_query).astype(jnp.float32).reshape(t, PEER_HEADS, 2, PEER_HALF)
        s = jnp.einsum('thpc,phkc->thpk', q, keys)
        sv, si = lax.top_k(s, PEER_TOPK)
        cand = (sv[:, :, 0, :, None] + sv[:, :, 1, None, :]).reshape(t, PEER_HEADS, PEER_TOPK * PEER_TOPK)
        cand_idx = (si[:, :, 0, :, None] * PEER_NKEYS + si[:, :, 1, None, :]).reshape(t, PEER_HEADS, PEER_TOPK * PEER_TOPK)
        top_s, top_pos = lax.top_k(cand, PEER_TOPK)
        idx = jnp.take_along_axis(cand_idx, top_pos, axis=-1).reshape(t, PEER_HEADS * PEER_TOPK)
        gate = jax.nn.softmax(top_s, axis=-1).reshape(t, PEER_HEADS * PEER_TOPK)
        u = expert_u[idx]
        act = jax.nn.gelu(jnp.einsum('tnd,td->tn', u, hb).astype(jnp.float32))
        return jnp.einsum('tn,tnd->td', (gate * act).astype(expert_v.dtype), expert_v[idx])

    y = lax.map(one_block, h)
    return y.reshape(b, lp, d).astype(x.dtype)

def setup_inputs(seed: int = 0) -> dict:
    key = jax.random.key(seed)
    ks = jax.random.split(key, 16)
    f32 = jnp.float32
    nrm = lambda k, shape, scale: jax.random.normal(k, shape, f32) * scale
    gain = lambda k, shape: 1.0 + 0.02 * jax.random.normal(k, shape, f32)
    return {
        'x': nrm(ks[0], (BATCH, SEQ, D_MODEL), 1.0),
        'meta_tokens': nrm(ks[1], (N_META, D_MODEL), 1.0),
        'even_norm_g': gain(ks[2], (N_EVEN, D_MODEL)),
        'even_w_in': nrm(ks[3], (N_EVEN, D_MODEL, IN_COLS), D_MODEL ** -0.5),
        'even_q_norm_g': gain(ks[4], (N_EVEN, SB_HEAD_DIM)),
        'even_k_norm_g': gain(ks[5], (N_EVEN, SB_HEAD_DIM)),
        'even_conv_w': nrm(ks[6], (N_EVEN, CONV_K, CONV_CH), CONV_K ** -0.5),
        'even_w_out': nrm(ks[7], (N_EVEN, SB_WIDTH + CONV_CH, D_MODEL), (SB_WIDTH + CONV_CH) ** -0.5),
        'odd_norm_g': gain(ks[8], (N_ODD, D_MODEL)),
        'odd_pool_w': nrm(ks[9], (N_ODD, len(POOL_WINDOWS), POOL_CH, POOL_CH), POOL_CH ** -0.5),
        'odd_pool_scale': gain(ks[10], (N_ODD, D_MODEL)),
        'ffn_norm_g': gain(ks[11], (DEPTH, D_MODEL)),
        'peer_w_query': nrm(ks[12], (DEPTH, D_MODEL, PEER_HEADS * 2 * PEER_HALF), D_MODEL ** -0.5),
        'peer_sub_keys': nrm(ks[13], (DEPTH, 2, PEER_HEADS, PEER_NKEYS, PEER_HALF), PEER_HALF ** -0.5),
        'peer_u': nrm(ks[14], (DEPTH, PEER_N, D_MODEL), D_MODEL ** -0.5),
        'peer_v': nrm(ks[15], (DEPTH, PEER_N, D_MODEL), PEER_HEADS ** -0.5),
    }

def reference(x, meta_tokens, even_norm_g, even_w_in, even_q_norm_g, even_k_norm_g, even_conv_w, even_w_out, odd_norm_g, odd_pool_w, odd_pool_scale, ffn_norm_g, peer_w_query, peer_sub_keys, peer_u, peer_v):
    b, seq, d = x.shape
    total = N_META + seq
    lp = -(-total // BLOCK_Q) * BLOCK_Q
    meta = jnp.broadcast_to(meta_tokens[None].astype(x.dtype), (b, N_META, d))
    h = jnp.concatenate([meta, x], axis=1)
    h = jnp.pad(h, ((0, 0), (0, lp - total), (0, 0)))
    for layer in range(DEPTH):
        i = layer // 2
        if layer % 2 == 0:
            h = h + even_layer(h, even_norm_g[i], even_w_in[i], even_q_norm_g[i], even_k_norm_g[i], even_conv_w[i], even_w_out[i])
        else:
            h = h + odd_layer(h, odd_norm_g[i], odd_pool_w[i], odd_pool_scale[i])
        h = h + peer_ffn(h, ffn_norm_g[layer], peer_w_query[layer], peer_sub_keys[layer], peer_u[layer], peer_v[layer])
    return h[:, N_META:N_META + seq]


_drawn_inputs = setup_inputs


def setup_inputs(seed=0):
    import zlib

    import numpy as np

    out = dict(_drawn_inputs(seed))
    spreads = {}
    factors = {'even_q_norm_g': 4.287,
     'even_k_norm_g': 3.897,
     'odd_norm_g': 10.816,
     'odd_pool_scale': 10.066,
     'ffn_norm_g': 2.998}
    for name, (base, spread) in spreads.items():
        noise = np.random.default_rng([zlib.crc32(name.encode()), seed]).standard_normal(out[name].shape)
        drawn = base * np.exp(spread * noise) if base else spread * noise
        out[name] = __import__('jax').numpy.asarray(drawn.astype(out[name].dtype))
    for name, factor in factors.items():
        out[name] = (out[name] * factor).astype(out[name].dtype)
    return out
```

```python
import numpy as np
import concourse.bass as bass
from concourse import mybir
from contextlib import ExitStack

F32 = mybir.dt.float32
BF16 = mybir.dt.bfloat16
U32 = mybir.dt.uint32
ALU = mybir.AluOpType
ACT = mybir.ActivationFunctionType
AX = mybir.AxisListType

P = 128
D = 1024
KD = D // P
META = 16
SEQ = 512
XT = SEQ // P
TILES = XT + 1
HEADS = 8
DH = 64
CONV = 512
GROUP = 512
EPS = 1e-6
NKEYS = 128
TOPK = 16
EXPERTS = NKEYS * NKEYS
CHUNK = 16
TILE_CHUNKS = P // CHUNK
PAIRS = TILE_CHUNKS // 2
CHUNKS = 1 + 2 * XT * TILE_CHUNKS
U_SLOTS = 4
V_SLOTS = 4
W_SLOTS = 4
LISTS = 4
WINDOWS = (2, 4, 8, 16)
PARTS = 3
BIG = 1e30
GELU_A = 2 * 0.7978845608028654
GELU_B = GELU_A * 0.044715


class Steps:

    def __init__(self, eng, sem, base=0):
        self.eng, self.sem, self.base, self.n = eng, sem, base, 0

    def did(self, ins):
        ins.then_inc(self.sem, 1)
        self.n += 1

    def settle(self):
        self.eng.wait_ge(self.sem, self.base + self.n)


def wait(eng, sem, value):
    if not (isinstance(value, int) and value <= 0):
        eng.wait_ge(sem, value)


def apart(eng):
    eng.nop(nofuse=True)


def rows_of(tile):
    return META if tile == XT else P


def cols_of(tile):
    return slice(SEQ, SEQ + META) if tile == XT else slice(P * tile, P * tile + P)


def program(nc, x, meta_tokens, even_norm_g, even_w_in, even_q_norm_g, even_k_norm_g, even_conv_w,
            even_w_out, odd_norm_g, odd_pool_w, odd_pool_scale, ffn_norm_g, peer_w_query,
            peer_sub_keys, peer_u, peer_v, out):
    ctx = ExitStack()
    mixer = ExitStack()
    with ctx:
        def sem(name):
            return ctx.enter_context(nc.semaphore(name))

        def sb(name, shape, dt=F32, where=ctx):
            return where.enter_context(nc.sbuf_tensor(name, shape, dt))

        hres = sb("hres", [P, TILES, D])
        ident = sb("ident", [P, P])
        eps_col = sb("eps_col", [P, 1])
        ss = sb("ss", [P, TILES])
        rstd = sb("rstd", [P, TILES])
        nt_a = sb("newton_a", [P, 80])
        nt_b = sb("newton_b", [P, 80])
        psum = ctx.enter_context(nc.psum_tensor("psum", [P, 8, 512], F32))

        with mixer:
            def sbm(name, shape, dt=F32):
                return sb(name, shape, dt, mixer)
            hT = sbm("hT", [P, KD, SEQ + META])
            xn = sbm("xn", [P, 2, D])
            gate_b = sbm("gate_b", [P, 4, META + SEQ])
            conv_in = sbm("conv_in", [P, 4, 2 + META + SEQ])
            conv_y = sbm("conv_y", [P, META + SEQ])
            qkv = sbm("qkv", [P, TILES, 3, GROUP])
            w_ring = sbm("w_ring", [P, 2, KD, GROUP])
            catT = sbm("catT", [P, KD, SEQ + META])
            qs = [sbm(f"qs{i}", [P, TILES, DH]) for i in range(2)]
            ks = [sbm(f"ks{i}", [P, TILES, DH]) for i in range(2)]
            vs = [sbm(f"vs{i}", [P, TILES, DH]) for i in range(2)]
            qT = [sbm(f"qT{i}", [DH, SEQ + META]) for i in range(2)]
            kT = [sbm(f"kT{i}", [DH, SEQ + P]) for i in range(2)]
            sp = [sbm(f"softplus{i}", [P, 4, 512]) for i in range(2)]
            wts = sbm("wts", [P, 4, 512])
            ssqk = sbm("ssqk", [P, TILES, 16])
            rqk = sbm("rqk", [P, TILES, 16])
            even_g = sbm("even_g", [P, KD])
            qg = sbm("qg", [DH, 1])
            qg8 = sbm("qg8", [DH, 1])
            kg = sbm("kg", [DH, 1])
            conv_w = sbm("conv_w", [P, 3, 4])
            causal = sbm("causal", [P, P])
            neg = sbm("neg", [P, P])
            neg_tri = sbm("neg_tri", [P, P])
            neg_ones = sbm("neg_ones", [P, P])
            w_out_sb = w_ring[:, :, :, :].rearrange("p a k n -> p (a k n)").rearrange("p (k n) -> p k n", k=KD)

        wq = sb("wq", [P, KD, 2 * D])
        WQ_EARLY = 5
        keysT = sb("keysT", [P, 2 * HEADS, NKEYS])
        u_ring = sb("u_ring", [P, U_SLOTS, D])
        v_ring = sb("v_ring", [P, V_SLOTS, D])
        hb = sb("hb", [P, D])
        hbT = sb("hbT", [P, KD, P])
        part = [sb(f"part{i}", [P, D], BF16) for i in range(PARTS)]
        hparts = sb("hparts", [PARTS * CHUNK, 2, D], BF16)
        pick = sb("pick", [PARTS * CHUNK, CHUNK, P], BF16)
        ffn_g = sb("ffn_g", [P, D])
        odd_g = sb("odd_g", [P, D])
        pool_s = sb("pool_s", [P, D])
        pool_w = sb("pool_w", [P, 4, 2, 256])
        prev = sb("prev", [P, D])
        band = sb("band", [P, 4, P])
        band_prev = sb("band_prev", [P, 4, P])
        q_sb = sb("q_sb", [P, 512])
        q_T = sb("q_T", [P, LISTS, P])
        work = sb("work", [P, 512])
        cand = sb("cand", [P, 512])
        sv = sb("sv", [P, LISTS, TOPK])
        si = sb("si", [P, LISTS, TOPK], U32)
        sif = sb("sif", [P, LISTS, TOPK])
        tv = sb("tv", [P, 2, TOPK])
        tpos = sb("tpos", [P, 2, TOPK], U32)
        ta = sb("ta", [P, 2, TOPK], U32)
        tb = sb("tb", [P, 2, TOPK], U32)
        ia = sb("ia", [P, 2, TOPK])
        ib = sb("ib", [P, 2, TOPK])
        iota16 = sb("iota16", [P, TOPK])
        top_s = sb("top_s", [P, P])
        top_i = sb("top_i", [P, P])
        soft = sb("soft", [P, P])
        soft_sum = sb("soft_sum", [P, HEADS])
        soft_r = sb("soft_r", [P, HEADS])
        idxT = sb("idxT", [P, CHUNKS * CHUNK], U32)
        gateT = sb("gateT", [P, CHUNKS * CHUNK])
        idx_u = [sb(f"idx_u{i}", [P, CHUNK], U32) for i in range(2)]
        idx_v = [sb(f"idx_v{i}", [P, CHUNK], U32) for i in range(2)]
        dot = [sb(f"dot{i}", [P, CHUNK]) for i in range(2)]
        weight = [sb(f"weight{i}", [P, CHUNK]) for i in range(2)]
        ga = sb("ga", [P, CHUNK])
        gb_ = sb("gb", [P, CHUNK])
        ge = sb("ge", [P, CHUNK])
        gx = sb("gx", [P, CHUNK])
        strip = sb("strip", [P, 2 * P - 1])
        w_col = sb("w_col", [P, W_SLOTS, P])
        zeros = sb("zeros", [P, 512], BF16)
        parts_dram = nc.dram_tensor("parts_dram", [CHUNKS, PARTS, CHUNK, D], BF16, kind="Internal").ap()

        bc = [psum[:, 0:2, :], psum[:, 2:4, :]]
        y_ps = psum[:, 4:6, :]
        FA, FB = psum[:, 6, :], psum[:, 7, :]

        s_x = [sem(f"x_loaded{t}") for t in range(TILES)]
        s_small = sem("small_loaded")
        s_win = [sem(f"w_in_loaded{i}") for i in range(2)]
        s_wout = sem("w_out_loaded")
        s_const = sem("mixer_constants_step")
        s_setup = sem("expert_constants_step")
        s_act = sem("act_step")
        s_dve = sem("dve_step")
        s_ss = sem("squares_summed")
        s_rstd = sem("rstd_ready")
        s_xn = sem("xn_ready")
        s_xnT = sem("xn_transposed")
        s_hT = sem("hT_ready")
        s_qkv_ps = sem("qkv_multiplied")
        s_qkv = sem("qkv_copied")
        s_fm_ps = sem("conv_inputs_multiplied")
        s_fm_a = sem("conv_gates_copied")
        s_fm_u = sem("conv_u_used")
        s_ssqk = sem("qk_squares_summed")
        s_rqk0 = sem("qk_rstd_guessed")
        s_rqk = sem("qk_rstd_ready")
        s_conv = sem("conv_done")
        s_qk_in = sem("head_qk_scaled")
        s_v_in = sem("head_v_copied")
        s_qkT_ps = sem("head_qk_transposed")
        s_qkT = sem("head_qkT_copied")
        s_z = sem("scores_ready")
        s_log = sem("log_terms_ready")
        s_sp = sem("softplus_ready")
        s_S = sem("log_weights_ready")
        s_w = sem("weights_ready")
        s_av = sem("head_attended")
        s_att = sem("head_copied")
        s_proj = sem("out_projected")
        s_mix = sem("mixer_added")

        s_wq = sem("w_query_loaded")
        s_keys_raw = sem("keys_loaded")
        s_keys_ps = sem("keys_transposed")
        s_keys = sem("keys_copied")
        s_ffng = sem("ffn_gain_loaded")
        s_oddw = sem("odd_weights_loaded")
        s_hsq = sem("h_squares_step")
        s_hguess = sem("h_rstd_guessed")
        s_hnewton = sem("h_newton_step")
        s_hb = sem("hb_ready")
        s_hbT_ps = sem("hb_transposed")
        s_hbT = sem("hbT_copied")
        s_split = sem("hb_split_step")
        s_parts = sem("hb_parts_ready")
        s_saved = sem("hb_parts_saved")
        s_fetched = [sem(f"chunk_parts_fetched{i}") for i in range(2)]
        s_q_ps = sem("query_multiplied")
        s_q = sem("query_copied")
        s_qT_ps = sem("query_transposed")
        s_qT = sem("queryT_copied")
        s_sc = sem("key_scores_ready")
        s_topk = sem("topk_step")
        s_routed = sem("two_heads_routed")
        s_tail = sem("gate_step")
        s_exp_in = sem("gate_logits_ready")
        s_exp = sem("gate_exponentials_ready")
        s_gate = sem("gates_ready")
        s_gateT = sem("gates_transposed")
        s_idx = sem("tile_routed")
        s_pool = sem("pool_step")
        s_psq = sem("pool_squares_step")
        s_pguess = sem("pool_rstd_guessed")
        s_hf = sem("pool_input_ready")
        s_dT_ps = sem("pool_differences_ready")
        s_dT = sem("pool_differences_copied")
        s_prev = sem("previous_rows_kept")
        s_py = sem("pool_multiplied")
        s_padd = sem("pool_added")

        s_idx_u = sem("u_indices_staged")
        s_idx_v = sem("v_indices_staged")
        s_u = [sem(f"u_rows_landed{i}") for i in range(U_SLOTS)]
        s_v = [sem(f"v_rows_landed{i}") for i in range(V_SLOTS)]
        s_bc = sem("token_row_broadcast")
        s_dot = sem("token_dotted")
        s_gelu = sem("gelu_step")
        s_garg = sem("gelu_argument_ready")
        s_gexp = sem("gelu_exponential_ready")
        s_weight = sem("expert_weights_ready")
        s_wcol = sem("weight_column_ready")
        s_acc = sem("token_accumulated")
        s_y = sem("tile_summed")
        s_yadd = sem("tile_added")
        s_out = sem("output_stored")

        KEY_BLOCKS = [3, 2, 1, 0]
        Z_AT = {3: (0, 0), 2: (0, P), 1: (1, 0), 0: (2, 0), XT: (3, 0)}
        Z_META = (1, 384)
        SEGMENTS = [(slice(0, 1), 0, 384), (slice(1, 2), 0, 400), (slice(2, 4), 0, 512)]

        def z_cols(t, b):
            bank, at = Z_AT[b]
            return t[:, bank, at:at + (512 if b == XT else SEQ - P * b)]

        NEWTON = 4
        SPLIT = 4
        TOPK_STEPS = 34
        GATE_STEPS = 2
        POOL_STEPS = NEWTON + 1
        GELU1, GELU2 = 3, 3

        def newton(dve, steps, guess, total, n, result, last):
            w = guess.shape[-1]
            a, b = nt_a[0:guess.shape[0], 0:w], nt_b[0:guess.shape[0], 0:w]
            steps.did(nc.vector.tensor_scalar(a, total, 1.0 / n, EPS, ALU.mult, ALU.add))
            steps.did(nc.vector.tensor_tensor(b, guess, guess, ALU.mult))
            steps.settle()
            steps.did(nc.vector.tensor_tensor(b, b, a, ALU.mult))
            steps.settle()
            steps.did(nc.vector.tensor_scalar(b, b, -0.5, 1.5, ALU.mult, ALU.add))
            steps.settle()
            nc.vector.tensor_tensor(result, guess, b, ALU.mult).then_inc(last, 1)

        def mixer_sync(sp_):
            for t in range(XT):
                sp_.dma_start(hres[:, t, :], x[0, P * t:P * t + P, :]).then_inc(s_x[t], 16)
            sp_.dma_start(hres[0:META, XT, :], meta_tokens[:, :]).then_inc(s_x[XT], 16)
            w_in = even_w_in[0].rearrange("(k p) n -> p k n", p=P)
            for g in range(6):
                if g >= 2:
                    if g - 2 < 3:
                        sp_.wait_ge(s_qkv_ps, TILES * (g - 1))
                    else:
                        sp_.wait_ge(s_fm_ps, 4 * (g - 4))
                sp_.dma_start(w_ring[:, g % 2, :, :], w_in[:, :, GROUP * g:GROUP * g + GROUP]).then_inc(s_win[g % 2], 16)
                if g == 0:
                    sp_.dma_start(even_g[:, :], even_norm_g[0].rearrange("(k p) -> p k", p=P), allow_slow_non_contiguous=True).then_inc(s_small, 16)
                    sp_.dma_start(qg[:, :], even_q_norm_g[0].rearrange("(p a) -> p a", a=1),
                                  allow_slow_non_contiguous=True).then_inc(s_small, 16)
                    sp_.dma_start(kg[:, :], even_k_norm_g[0].rearrange("(p a) -> p a", a=1),
                                  allow_slow_non_contiguous=True).then_inc(s_small, 16)
                    for i in range(3):
                        sp_.dma_start(conv_w[:, i, :], even_conv_w[0, i].rearrange("(m p) -> p m", p=P),
                                      allow_slow_non_contiguous=True).then_inc(s_small, 16)
            sp_.wait_ge(s_fm_ps, 12)
            sp_.dma_start(w_out_sb, even_w_out[0].rearrange("(k p) n -> p k n", p=P)).then_inc(s_wout, 16)
        SMALL = 6 * 16

        def wq_sync(sp_, layer, k0, k1):
            if layer == 0:
                if k0 == 0:
                    sp_.wait_ge(s_fm_ps, 12)
                    sp_.wait_ge(s_conv, 8)
                    sp_.wait_ge(s_ssqk, TILES)
                else:
                    sp_.wait_ge(s_qk_in, 2 * HEADS)
                    sp_.wait_ge(s_v_in, HEADS)
            elif k0 == 0:
                sp_.wait_ge(s_q_ps, PAIRS * 5)
            w = peer_w_query[layer].rearrange("(k p) n -> p k n", p=P)
            for k in range(k0, k1):
                sp_.dma_start(wq[:, k, :], w[:, k, :]).then_inc(s_wq, 16)

        def keys_sync(sp_, layer, half):
            if half == 0:
                if layer == 0:
                    sp_.wait_ge(s_mix, 2 * TILES)
                    sp_.wait_ge(s_proj, 2 * TILES)
                else:
                    sp_.wait_ge(s_q_ps, PAIRS * 5)
                    sp_.wait_ge(s_hb, 5)
                sp_.dma_start(ffn_g[:, :], ffn_norm_g[layer:layer + 1, :].broadcast_to([P, D])).then_inc(s_ffng, 16)
            else:
                sp_.wait_ge(s_keys_ps, 2 * layer + 1)
            for p_ in range(2):
                sp_.dma_start(hbT[:, 4 * p_:4 * p_ + 4, :],
                              peer_sub_keys[layer, p_, 4 * half:4 * half + 4, :, :].rearrange("h k c -> k h c")
                              ).then_inc(s_keys_raw, 16)

        def odd_weights_sync(sp_):
            sp_.dma_start(odd_g[:, :], odd_norm_g[0:1, :].broadcast_to([P, D])).then_inc(s_oddw, 16)
            sp_.dma_start(pool_s[:, :], odd_pool_scale[0:1, :].broadcast_to([P, D])).then_inc(s_oddw, 16)
            for g in range(4):
                sp_.dma_start(pool_w[:, g, :, :], odd_pool_w[0, g].rearrange("(k p) n -> p k n", p=P)).then_inc(s_oddw, 16)
        ODD_LOADS = 6 * 16

        def save_parts(sp_, job, chunk, n_tokens):
            sp_.wait_ge(s_parts, job + 1)
            n = n_tokens // CHUNK
            for i in range(PARTS):
                sp_.dma_start(parts_dram[bass.ds(chunk, n), i, :, :], part[i][0:n_tokens, :]).then_inc(s_saved, 16)
            sp_.wait_ge(s_saved, 16 * PARTS * (job + 1))
            apart(sp_)

        def fetch_parts(sp_, u, par):
            wait(sp_, s_dot, CHUNK * (u - 1))
            sp_.dma_start(hparts[:, par, :], parts_dram[bass.ds(u, 1), :, :, :].rearrange("u a t d -> (u a t) d")).then_inc(s_fetched[par], 16)

        def mixer_constants(pool):
            c = Steps(pool, s_const)
            c.did(nc.gpsimd.memset(ident[:, :], 0.0))
            c.did(nc.gpsimd.memset(eps_col[:, :], EPS))
            c.did(nc.gpsimd.memset(causal[:, :], 1.0))
            c.did(nc.gpsimd.memset(neg[:, :], 0.0))
            c.did(nc.gpsimd.memset(neg_tri[:, :], -1.0))
            c.did(nc.gpsimd.memset(neg_ones[:, :], -1.0))
            c.did(nc.gpsimd.memset(kT[0][:, :], 0.0))
            c.did(nc.gpsimd.memset(kT[1][:, :], 0.0))
            c.did(nc.gpsimd.memset(ss[:, :], 1.0))
            c.did(nc.gpsimd.memset(ssqk[:, :, :], 1.0))
            c.did(nc.gpsimd.memset(qkv[:, XT, :, :], 0.0))
            c.did(nc.gpsimd.memset(conv_in[:, :, 0:2], 0.0))
            c.settle()
            c.did(nc.gpsimd.affine_select(out=ident[:, :], in_=ident[:, :], compare_op=ALU.not_equal, fill=1.0,
                                          base=0, pattern=[[-1, P]], channel_multiplier=1))
            c.did(nc.gpsimd.affine_select(out=causal[:, :], in_=causal[:, :], compare_op=ALU.is_gt, fill=0.0,
                                          base=0, pattern=[[1, P]], channel_multiplier=-1))
            c.did(nc.gpsimd.affine_select(out=neg[:, :], in_=neg[:, :], compare_op=ALU.is_gt, fill=-BIG,
                                          base=0, pattern=[[1, P]], channel_multiplier=-1))
            c.did(nc.gpsimd.affine_select(out=neg_tri[:, :], in_=neg_tri[:, :], compare_op=ALU.is_ge, fill=0.0,
                                          base=0, pattern=[[-1, P]], channel_multiplier=1))
            return c.n
        MIXER_CONSTANTS = 16

        def expert_constants(pool):
            pool.wait_ge(s_mix, 2 * TILES)
            pool.wait_ge(s_proj, 2 * TILES)
            c = Steps(pool, s_setup)
            c.did(nc.gpsimd.memset(pick[:, :, :], 0.0))
            c.did(nc.gpsimd.memset(strip[:, :], 0.0))
            c.did(nc.gpsimd.memset(zeros[:, :], 0.0))
            c.did(nc.gpsimd.memset(prev[:, :], 0.0))
            c.did(nc.gpsimd.iota(iota16[:, :], pattern=[[1, TOPK]], base=0, channel_multiplier=0,
                                 allow_small_or_imprecise_dtypes=True))
            for g, w in enumerate(WINDOWS):
                c.did(nc.gpsimd.memset(band[:, g, :], 1.0 / w))
                c.did(nc.gpsimd.memset(band_prev[:, g, :], 1.0 / w))
            c.settle()
            c.did(nc.gpsimd.affine_select(out=strip[:, :], in_=strip[:, :], compare_op=ALU.not_equal, fill=1.0,
                                          base=-(P - 1), pattern=[[1, 2 * P - 1]], channel_multiplier=0))
            for g, w in enumerate(WINDOWS):
                c.did(nc.gpsimd.affine_select(out=band[:, g, :], in_=band[:, g, :], compare_op=ALU.is_ge, fill=0.0,
                                              base=0, pattern=[[1, P]], channel_multiplier=-1))
                c.did(nc.gpsimd.affine_select(out=band_prev[:, g, :], in_=band_prev[:, g, :], compare_op=ALU.is_ge,
                                              fill=0.0, base=w - 1 - P, pattern=[[-1, P]], channel_multiplier=1))
            for i in range(PARTS):
                c.settle()
                c.did(nc.gpsimd.affine_select(out=pick[:, :, :], in_=pick[:, :, :], compare_op=ALU.not_equal, fill=1.0,
                                              base=-CHUNK * i, pattern=[[-1, CHUNK], [0, P]], channel_multiplier=1))
            c.settle()
            for g, w in enumerate(WINDOWS):
                c.did(nc.gpsimd.affine_select(out=band[:, g, :], in_=band[:, g, :], compare_op=ALU.is_ge, fill=0.0,
                                              base=w - 1, pattern=[[-1, P]], channel_multiplier=1))
            c.settle()
            for g in range(4):
                c.did(nc.gpsimd.tensor_tensor(band[:, g, :], band[:, g, :], ident[:, :], ALU.subtract))
            assert c.n == SETUP_STEPS, c.n
        SETUP_STEPS = 5 + 8 + 1 + 8 + PARTS + 4 + 4

        def mixer_tensor(pe):
            pe.wait_ge(s_const, MIXER_CONSTANTS)
            for i, t in enumerate(range(TILES)):
                n = rows_of(t)
                pe.wait_ge(s_xn, i + 1)
                if i >= 2:
                    pe.wait_ge(s_hT, 2 * (i - 1))
                for k in range(KD):
                    last = nc.tensor.transpose(psum[:, 2 * (i % 2) + k // 4, n * (k % 4):n * (k % 4) + n],
                                               xn[0:n, i % 2, P * k:P * k + P], ident[0:n, 0:n])
                last.then_inc(s_xnT, 1)
            pe.wait_ge(s_hT, 2 * TILES)
            for g in range(3):
                pe.wait_ge(s_win[g % 2], 16 * (g // 2 + 1))
                for t in range(TILES):
                    i = TILES * g + t
                    if i >= 4:
                        pe.wait_ge(s_qkv, i - 3)
                    n = rows_of(t)
                    for k in range(KD):
                        last = nc.tensor.matmul(psum[0:n, 4 + i % 4, :], hT[:, k, cols_of(t)], w_ring[:, g % 2, k, :],
                                                start=(k == 0), stop=(k == KD - 1))
                    last.then_inc(s_qkv_ps, 1)
            pe.wait_ge(s_qkv, 3 * TILES)
            for g in range(3):
                pe.wait_ge(s_win[(g + 3) % 2], 16 * ((g + 3) // 2 + 1))
                for m in range(4):
                    i = 4 * g + m
                    if i >= 2:
                        if i - 2 < 8:
                            pe.wait_ge(s_fm_a, 2 * (i - 1))
                        else:
                            pe.wait_ge(s_fm_u, 2 * (i - 2 - 7))
                    for k in range(KD):
                        w = w_ring[:, (g + 3) % 2, k, P * m:P * m + P]
                        nc.tensor.matmul(psum[:, 4 + 2 * (i % 2), :], w, hT[:, k, 0:SEQ], start=(k == 0), stop=(k == KD - 1))
                        last = nc.tensor.matmul(psum[:, 5 + 2 * (i % 2), 0:META], w, hT[:, k, SEQ:SEQ + META],
                                                start=(k == 0), stop=(k == KD - 1))
                    last.then_inc(s_fm_ps, 1)
            pe.wait_ge(s_fm_u, 8)

            def transpose_qk(h, par):
                pe.wait_ge(s_qk_in, 2 * h + 2)
                pe.wait_ge(s_v_in, h + 1)
                apart(pe)
                for i, src in enumerate((qs[par], ks[par])):
                    for t in range(TILES):
                        n = rows_of(t)
                        bank = 4 * par + 2 * i + t // XT
                        at = P * (t % XT)
                        last = nc.tensor.transpose(psum[0:DH, bank, at:at + n], src[0:n, t, :], ident[0:n, 0:n])
                last.then_inc(s_qkT_ps, 1)

            def scores(h, par):
                pe.wait_ge(s_qkT, 4 * h + 4)
                for b in KEY_BLOCKS + [XT]:
                    bank, at = Z_AT[b]
                    q0 = 0 if b == XT else P * b
                    nc.tensor.matmul(psum[:, 4 * par + bank, at:at + SEQ - q0], kT[par][:, P * b:P * b + P],
                                     qT[par][:, q0:SEQ], start=(at == 0), stop=True, skip_group_check=True)
                nc.tensor.matmul(psum[:, 4 * par + Z_META[0], Z_META[1]:Z_META[1] + META], kT[par][:, SEQ:SEQ + P],
                                 qT[par][:, SEQ:SEQ + META], start=False, stop=True,
                                 skip_group_check=True).then_inc(s_z, 1)

            def subtract_later(h, par):
                pe.wait_ge(s_sp, h + 1)
                for b in KEY_BLOCKS + [XT]:
                    bank, at = Z_AT[b]
                    bank += 4 * par
                    rows = META if b == XT else P
                    q0 = 0 if b == XT else P * b

                    def add(cols, lhsT, rhs):
                        return nc.tensor.matmul(psum[:, bank, cols], lhsT, rhs, start=False, stop=True, skip_group_check=True)
                    add(slice(at, at + SEQ - q0), neg_tri[0:rows, :], z_cols(sp[par], b)[0:rows, :])
                    for c in [c for c in KEY_BLOCKS if b == XT or c > b]:
                        add(slice(at + P * c - q0, at + SEQ - q0), neg_ones[:, :], z_cols(sp[par], c))
                    if b != XT:
                        add(slice(at, at + P), ident[:, :], neg[:, :])
                bank, at = 4 * par + Z_META[0], Z_META[1]
                nc.tensor.matmul(psum[:, bank, at:at + META], neg_tri[0:META, :], sp[par][0:META, Z_META[0], at:at + META],
                                 start=False, stop=True, skip_group_check=True)
                nc.tensor.matmul(psum[:, bank, at:at + META], ident[:, :], neg[:, 0:META], start=False, stop=True,
                                 skip_group_check=True).then_inc(s_S, 1)

            def attend(h, par):
                pe.wait_ge(s_w, h + 1)
                pe.wait_ge(s_v_in, h + 1)
                nc.tensor.matmul(psum[0:DH, 4 * par, :], vs[par][0:META, XT, :], wts[0:META, 3, :], start=True, stop=True)
                for b in range(XT):
                    nc.tensor.matmul(psum[0:DH, 4 * par, P * b:SEQ], vs[par][:, b, :], z_cols(wts, b), start=False,
                                     stop=True, skip_group_check=True)
                nc.tensor.matmul(psum[0:DH, 4 * par + 1, 0:META], vs[par][0:META, XT, :],
                                 wts[0:META, Z_META[0], Z_META[1]:Z_META[1] + META], start=True, stop=True).then_inc(s_av, 1)

            transpose_qk(0, 0)
            scores(0, 0)
            with pe.Fori(0, HEADS // 2 - 1) as pair:
                for hh in range(2):
                    h = 2 * pair + hh
                    transpose_qk(h + 1, 1 - hh)
                    subtract_later(h, hh)
                    scores(h + 1, 1 - hh)
                    attend(h, hh)
            for h in (HEADS - 2, HEADS - 1):
                if h + 1 < HEADS:
                    transpose_qk(h + 1, (h + 1) % 2)
                subtract_later(h, h % 2)
                if h + 1 < HEADS:
                    scores(h + 1, (h + 1) % 2)
                attend(h, h % 2)
            pe.wait_ge(s_att, 2 * HEADS)
            pe.wait_ge(s_conv, 8)
            pe.wait_ge(s_wout, 16)
            for t in range(TILES):
                n = rows_of(t)
                for half in range(2):
                    i = 2 * t + half
                    if i >= 4:
                        pe.wait_ge(s_mix, i - 3)
                    for k in range(KD):
                        last = nc.tensor.matmul(psum[0:n, i % 4, :], catT[:, k, cols_of(t)],
                                                w_out_sb[:, k, 512 * half:512 * half + 512],
                                                start=(k == 0), stop=(k == KD - 1))
                    last.then_inc(s_proj, 1)

        def mixer_scalar(act):
            nc.scalar.preload_act_table_set("natural_log_exp_and_others")
            act.wait_ge(s_const, MIXER_CONSTANTS)
            a = Steps(act, s_act)
            for t in range(TILES):
                n = rows_of(t)
                act.wait_ge(s_x[t], 16)
                a.did(nc.scalar.activation(sp[t % 2][0:n, 0:2, :].rearrange("p a b -> p (a b)"),
                                           hres[0:n, t, :], ACT.Square, accum_out=ss[0:n, t:t + 1]))
                a.settle()
            a.did(nc.scalar.activation(rstd[:, :], ss[:, :], ACT.Ln, scale=1.0 / D, bias=eps_col[:, :]))
            a.settle()
            nc.scalar.activation(rstd[:, :], rstd[:, :], ACT.Exp, scale=-0.5).then_inc(s_ss, 1)
            for g in range(3):
                for t in range(TILES):
                    i = TILES * g + t
                    n = rows_of(t)
                    act.wait_ge(s_qkv_ps, i + 1)
                    nc.scalar.copy(qkv[0:n, t, g, :], psum[0:n, 4 + i % 4, :]).then_inc(s_qkv, 1)
            for i in range(8):
                act.wait_ge(s_fm_ps, i + 1)
                dst = gate_b[:, i, :] if i < 4 else conv_in[:, i - 4, 2:2 + META + SEQ]
                nc.scalar.copy(dst[:, META:META + SEQ], psum[:, 4 + 2 * (i % 2), :]).then_inc(s_fm_a, 1)
                nc.scalar.copy(dst[:, 0:META], psum[:, 5 + 2 * (i % 2), 0:META]).then_inc(s_fm_a, 1)
            act.wait_ge(s_ssqk, TILES)
            a.did(nc.scalar.activation(rqk[:, :, :], ssqk[:, :, :], ACT.Ln, scale=1.0 / DH, bias=eps_col[:, :]))
            a.settle()
            nc.scalar.activation(rqk[:, :, :], rqk[:, :, :], ACT.Exp, scale=-0.5).then_inc(s_rqk0, 1)

            def take_v(h, par):
                if not (isinstance(h, int) and h < 2):
                    act.wait_ge(s_av, h - 1)
                nc.scalar.copy(vs[par][:, :, :], qkv[:, :, 2, bass.ts(h, DH)]).then_inc(s_v_in, 1)

            def copy_qk(h, par):
                act.wait_ge(s_qkT_ps, h + 1)
                for i, (dst, gain) in enumerate(((qT[par], qg8), (kT[par], kg))):
                    bank = 4 * par + 2 * i
                    nc.scalar.activation(dst[:, 0:SEQ], psum[0:DH, bank, :], ACT.Copy, scale=gain[:, 0:1]).then_inc(s_qkT, 1)
                    nc.scalar.activation(dst[:, SEQ:SEQ + META], psum[0:DH, bank + 1, 0:META], ACT.Copy,
                                         scale=gain[:, 0:1]).then_inc(s_qkT, 1)

            def log_terms(h, par):
                act.wait_ge(s_z, h + 1)
                s = Steps(act, s_log, 9 * h)
                zs = psum[:, 4 * par:4 * par + 4, :]
                for func, src, kw in ((ACT.Abs, zs, {}), (ACT.Exp, sp[par], {"scale": -1.0}), (ACT.Ln, sp[par], {"bias": 1.0})):
                    for i, (banks, c0, c1) in enumerate(SEGMENTS):
                        if func != ACT.Abs:
                            act.wait_ge(s_log, s.base + s.n - 2)
                        s.did(nc.scalar.activation(sp[par][:, banks, c0:c1], src[:, banks, c0:c1], func, **kw))

            def weights(h, par):
                act.wait_ge(s_S, h + 1)
                for banks, c0, c1 in SEGMENTS:
                    ins = nc.scalar.activation(wts[:, banks, c0:c1], psum[:, banks.start + 4 * par:banks.stop + 4 * par, c0:c1], ACT.Exp)
                ins.then_inc(s_w, 1)

            def copy_out(h, par, block):
                act.wait_ge(s_av, h + 1)
                rows = slice(DH * par, DH * par + DH)
                nc.scalar.copy(catT[rows, block, 0:SEQ], psum[0:DH, 4 * par, :]).then_inc(s_att, 1)
                nc.scalar.copy(catT[rows, block, SEQ:SEQ + META], psum[0:DH, 4 * par + 1, 0:META]).then_inc(s_att, 1)

            take_v(0, 0)
            copy_qk(0, 0)
            log_terms(0, 0)
            take_v(1, 1)
            with act.Fori(0, HEADS // 2 - 1) as pair:
                for hh in range(2):
                    h = 2 * pair + hh
                    copy_qk(h + 1, 1 - hh)
                    weights(h, hh)
                    log_terms(h + 1, 1 - hh)
                    copy_out(h, hh, pair)
                    take_v(h + 2, hh)
            for h in (HEADS - 2, HEADS - 1):
                if h + 1 < HEADS:
                    copy_qk(h + 1, (h + 1) % 2)
                weights(h, h % 2)
                if h + 1 < HEADS:
                    log_terms(h + 1, (h + 1) % 2)
                copy_out(h, h % 2, h // 2)

        def mixer_vector(dve):
            dve.wait_ge(s_const, MIXER_CONSTANTS)
            d = Steps(dve, s_dve)
            dve.wait_ge(s_ss, 1)
            newton(dve, d, rstd[:, :], ss[:, :], D, rstd[:, :], s_rstd)
            dve.wait_ge(s_rstd, 1)
            dve.wait_ge(s_small, SMALL)
            for t in range(TILES):
                n = rows_of(t)
                dve.wait_ge(s_x[t], 16)
                if t >= 2:
                    dve.wait_ge(s_xnT, t - 1)
                nc.vector.tensor_scalar(xn[0:n, t % 2, :], hres[0:n, t, :], rstd[0:n, t:t + 1], None, ALU.mult).then_inc(s_xn, 1)
                dve.wait_ge(s_xnT, t + 1)
                for half in range(2):
                    nc.vector.tensor_tensor(hT[:, 4 * half:4 * half + 4, cols_of(t)],
                                            psum[:, 2 * (t % 2) + half, 0:4 * n].rearrange("p (k n) -> p k n", k=4),
                                            even_g[:, 4 * half:4 * half + 4].unsqueeze(2).to_broadcast([P, 4, n]),
                                            ALU.mult).then_inc(s_hT, 1)
            d.did(nc.vector.tensor_scalar(qg8[:, :], qg[:, :], DH ** -0.5, None, ALU.mult))
            dve.wait_ge(s_xnT, TILES)
            for t in range(TILES):
                n = rows_of(t)
                dve.wait_ge(s_qkv, TILES + t + 1)
                if t >= 2:
                    dve.wait_ge(s_ssqk, t - 1)
                qk = qkv[0:n, t, 0:2, :].rearrange("p a b -> p (a b)")
                d.did(nc.vector.tensor_tensor(xn[0:n, t % 2, :], qk, qk, ALU.mult))
                d.settle()
                nc.vector.tensor_reduce(ssqk[0:n, t, :], xn[0:n, t % 2, :].rearrange("p (h c) -> p h c", c=DH), AX.X,
                                        ALU.add).then_inc(s_ssqk, 1)
            dve.wait_ge(s_rqk0, 1)
            flat = rqk[:, :, :].rearrange("p a b -> p (a b)")
            newton(dve, d, flat, ssqk[:, :, :].rearrange("p a b -> p (a b)"), DH, flat, s_rqk)
            for m in range(4):
                dve.wait_ge(s_fm_a, 8 + 2 * m + 2)
                dve.wait_ge(s_fm_ps, 8 + m + 1)
                cin = conv_in[:, m, :]
                for c0, c1, src in ((META, META + SEQ, psum[:, 4 + 2 * (m % 2), :]), (0, META, psum[:, 5 + 2 * (m % 2), 0:META])):
                    nc.vector.tensor_tensor(cin[:, 2 + c0:2 + c1], cin[:, 2 + c0:2 + c1], src, ALU.mult).then_inc(s_fm_u, 1)
                dve.wait_ge(s_fm_u, 2 * m + 2)
                if m:
                    dve.wait_ge(s_conv, 2 * m)
                n = META + SEQ
                d.did(nc.vector.tensor_scalar(conv_y[:, :], cin[:, 0:n], conv_w[:, 0, m:m + 1], None, ALU.mult))
                d.settle()
                for i in (1, 2):
                    d.did(nc.vector.scalar_tensor_tensor(out=conv_y[:, :], in0=cin[:, i:i + n], scalar=conv_w[:, i, m:m + 1],
                                                         in1=conv_y[:, :], op0=ALU.mult, op1=ALU.add))
                    d.settle()
                nc.vector.tensor_tensor(catT[:, 4 + m, 0:SEQ], conv_y[:, META:n], gate_b[:, m, META:n], ALU.mult).then_inc(s_conv, 1)
                nc.vector.tensor_tensor(catT[:, 4 + m, SEQ:SEQ + META], conv_y[:, 0:META], gate_b[:, m, 0:META],
                                        ALU.mult).then_inc(s_conv, 1)
            dve.wait_ge(s_rqk, 1)
            before = d.n
            HEAD_STEPS = 3

            def scale_qk(h, par):
                if not (isinstance(h, int) and h < 2):
                    dve.wait_ge(s_qkT_ps, h - 1)
                for i, dst in enumerate((qs[par], ks[par])):
                    scale = rqk[:, :, bass.ds(h + HEADS * i, 1)].to_broadcast([P, TILES, DH])
                    nc.vector.tensor_tensor(dst[:, :, :], qkv[:, :, i, bass.ts(h, DH)], scale, ALU.mult).then_inc(s_qk_in, 1)

            def softplus(h, par):
                s = Steps(dve, s_dve, before + HEAD_STEPS * h)
                dve.wait_ge(s_log, 9 * h + 9)
                for banks, c0, c1 in SEGMENTS:
                    s.did(nc.vector.scalar_tensor_tensor(out=sp[par][:, banks, c0:c1],
                                                         in0=psum[:, banks.start + 4 * par:banks.stop + 4 * par, c0:c1], scalar=0.0,
                                                         in1=sp[par][:, banks, c0:c1], op0=ALU.max, op1=ALU.add))
                s.settle()
                for b in KEY_BLOCKS:
                    v = z_cols(sp[par], b)[:, 0:P]
                    nc.vector.tensor_tensor(v, v, causal[:, :], ALU.mult)
                v = sp[par][0:META, Z_META[0], Z_META[1]:Z_META[1] + META]
                nc.vector.tensor_tensor(v, v, causal[0:META, 0:META], ALU.mult).then_inc(s_sp, 1)
                assert s.n == HEAD_STEPS

            scale_qk(0, 0)
            scale_qk(1, 1)
            with dve.Fori(0, HEADS // 2 - 1) as pair:
                for hh in range(2):
                    softplus(2 * pair + hh, hh)
                    scale_qk(2 * pair + hh + 2, hh)
            softplus(HEADS - 2, 0)
            softplus(HEADS - 1, 1)
            for t in range(TILES):
                n = rows_of(t)
                for half in range(2):
                    i = 2 * t + half
                    dve.wait_ge(s_proj, i + 1)
                    v = hres[0:n, t, 512 * half:512 * half + 512]
                    nc.vector.tensor_tensor(v, v, psum[0:n, i % 4, :], ALU.add).then_inc(s_mix, 1)

        def keys_tensor(pe, layer, half):
            pe.wait_ge(s_keys_raw, 32 * (2 * layer + half + 1))
            wait(pe, s_keys, 2 * (2 * layer + half))
            if layer and not half:
                pe.wait_ge(s_routed, PAIRS * 5 + 1)
                pe.wait_ge(s_idx, 5)
            for i in range(8):
                last = nc.tensor.transpose((FA, FB)[i // 4][:, P * (i % 4):P * (i % 4) + P], hbT[:, i, :], ident[:, :])
            last.then_inc(s_keys_ps, 1)

        def keys_scalar(act, layer, half):
            lists = keysT[:, :, :].rearrange("c (h a) k -> c a h k", a=2)
            act.wait_ge(s_keys_ps, 2 * layer + half + 1)
            for p_ in range(2):
                nc.scalar.copy(lists[:, p_, 4 * half:4 * half + 4, :],
                               (FA, FB)[p_].rearrange("p (h k) -> p h k", h=4)).then_inc(s_keys, 1)

        def norm_scalar(act, job, n, src):
            wait(act, s_parts, job)
            wait(act, s_saved, 16 * PARTS * job)
            apart(act)
            nc.scalar.activation(part[0][0:n, :], src, ACT.Square, accum_out=ss[0:n, 0:1]).then_inc(s_hsq, 1)
            act.wait_ge(s_hsq, 2 * job + 1)
            nc.scalar.activation(rstd[0:n, 0:1], ss[0:n, 0:1], ACT.Ln, scale=1.0 / D, bias=eps_col[0:n, :]).then_inc(s_hsq, 1)
            act.wait_ge(s_hsq, 2 * job + 2)
            nc.scalar.activation(rstd[0:n, 0:1], rstd[0:n, 0:1], ACT.Exp, scale=-0.5).then_inc(s_hguess, 1)

        def transposed_scalar(act, job, n):
            act.wait_ge(s_hbT_ps, job + 1)
            for half in range(2):
                nc.scalar.copy(hbT[:, 4 * half:4 * half + 4, 0:n],
                               (FA, FB)[half][:, 0:4 * n].rearrange("p (k n) -> p k n", k=4)).then_inc(s_hbT, 1)

        def norm_vector(dve, job, n, src, layer):
            dve.wait_ge(s_hguess, job + 1)
            newton(dve, Steps(dve, s_hnewton, (NEWTON + 1) * job), rstd[0:n, 0:1], ss[0:n, 0:1], D, rstd[0:n, 0:1], s_hnewton)
            dve.wait_ge(s_hnewton, (NEWTON + 1) * (job + 1))
            dve.wait_ge(s_ffng, 16 * (layer + 1))
            nc.vector.scalar_tensor_tensor(out=hb[0:n, :], in0=src, scalar=rstd[0:n, 0:1], in1=ffn_g[0:n, :],
                                           op0=ALU.mult, op1=ALU.mult).then_inc(s_hb, 1)
            dve.wait_ge(s_hb, job + 1)

        def split_vector(dve, job, n, step):
            if step == 1:
                dve.wait_ge(s_hbT_ps, job + 1)
            if step:
                dve.wait_ge(s_split, SPLIT * job + step)
            if step % 2 == 0:
                nc.vector.tensor_copy(part[step // 2][0:n, :], hb[0:n, :]).then_inc(s_split if step < SPLIT else s_parts, 1)
            else:
                nc.vector.tensor_tensor(hb[0:n, :], hb[0:n, :], part[step // 2][0:n, :], ALU.subtract).then_inc(s_split, 1)

        def start_tensor(pe, job, n, layer):
            pe.wait_ge(s_hb, job + 1)
            pe.wait_ge(s_keys, 4 * (layer + 1))
            pe.wait_ge(s_wq, 16 * KD * (layer + 1))
            pe.wait_ge(s_routed, PAIRS * job + 1)
            wait(pe, s_idx, job)
            wait(pe, s_hbT, 2 * job)
            wait(pe, s_qT, PAIRS * job)
            for k in range(KD):
                last = nc.tensor.transpose((FA, FB)[k // 4][:, n * (k % 4):n * (k % 4) + n], hb[0:n, P * k:P * k + P],
                                           ident[0:n, 0:n])
            last.then_inc(s_hbT_ps, 1)

        def query_tensor(pe, piece, s, n, k0, k1, dst):
            for k in range(k0, k1):
                ins = nc.tensor.matmul(dst[0:n, :], hbT[:, k, 0:n], wq[:, k, bass.ts(s, 512)],
                                       start=(k == 0), stop=(k == KD - 1))
            if k1 == KD:
                ins.then_inc(s_q_ps, 1)

        def query_scalar(act, piece, n, src):
            act.wait_ge(s_q_ps, piece + 1)
            nc.scalar.copy(q_sb[0:n, :], src[0:n, :]).then_inc(s_q, 1)

        def queryT_tensor(pe, piece, n):
            pe.wait_ge(s_q, piece + 1)
            apart(pe)
            for i in range(LISTS):
                last = nc.tensor.transpose(FB[:, n * i:n * i + n], q_sb[0:n, P * i:P * i + P], ident[0:n, 0:n])
            last.then_inc(s_qT_ps, 1)

        def queryT_scalar(act, piece, n):
            act.wait_ge(s_qT_ps, piece + 1)
            nc.scalar.copy(q_T[:, :, 0:n], FB[:, 0:LISTS * n].rearrange("p (a n) -> p a n", a=LISTS)).then_inc(s_qT, 1)

        def free_tensor(pe, piece):
            wait(pe, s_read, piece)

        def scores_tensor(pe, piece, s, n):
            pe.wait_ge(s_qT, piece + 1)
            for i in range(LISTS):
                lists = keysT[:, bass.ds(LISTS * s + i, 1), :].rearrange("p a k -> p (a k)")
                last = nc.tensor.matmul(FA[0:n, P * i:P * i + P], q_T[:, i, 0:n], lists, start=True, stop=True)
            last.then_inc(s_sc, 1)
        s_read = sem("key_scores_read")
        s_routed_in = sem("key_numbers_as_floats")
        s_onehot = sem("onehot_step")

        def topk_stages(dve, piece, s, n):
            c = Steps(dve, s_topk, TOPK_STEPS * piece)
            e = Steps(dve, s_onehot, 8 * piece)
            r = slice(0, n)
            lists = [FA[r, P * i:P * i + P] for i in range(LISTS)]
            works = [work[r, P * i:P * i + P] for i in range(LISTS)]
            cands = [cand[r, 256 * h:256 * h + 256] for h in range(2)]
            cworks = [work[r, 256 * h:256 * h + 256] for h in range(2)]
            cand4 = cand[r, :].rearrange("p (h a b) -> p h a b", h=2, a=TOPK)
            work4 = work[r, :].rearrange("p (h a b) -> p h a b", h=2, a=TOPK)

            def best8(vals, src):
                c.settle()
                apart(dve)
                for i in range(len(src)):
                    c.did(nc.vector.max(vals[r, i, 0:8], src[i]))

            def numbers8(vals, idx, src, dst, done=None):
                c.settle()
                apart(dve)
                for i in range(len(src)):
                    c.did(nc.vector.max_index(idx[r, i, 0:8], vals[r, i, 0:8], src[i]))
                for i in range(len(src)):
                    ins = nc.vector.match_replace(dst[i], vals[r, i, 0:8], src[i], -3e38)
                    if done is not None and i == len(src) - 1:
                        ins.then_inc(done, 1)
                    else:
                        c.did(ins)

            def next8(vals, dst):
                c.settle()
                apart(dve)
                for i in range(len(dst)):
                    c.did(nc.vector.max(vals[r, i, 8:16], dst[i]))

            def next_numbers8(vals, idx, dst):
                c.settle()
                apart(dve)
                for i in range(len(dst)):
                    c.did(nc.vector.max_index(idx[r, i, 8:16], vals[r, i, 8:16], dst[i]))

            def lists_best():
                dve.wait_ge(s_sc, piece + 1)
                apart(dve)
                for i in range(LISTS):
                    c.did(nc.vector.max(sv[r, i, 0:8], lists[i]))

            def lists_numbers():
                numbers8(sv, si, lists, works, s_read)
                dve.wait_ge(s_read, piece + 1)

            def sums():
                c.settle()
                v = sv[r, :, :].rearrange("p (h a) k -> p h a k", a=2)
                for h in range(2):
                    c.did(nc.vector.tensor_tensor(cand4[:, h], v[:, h, 0, :].unsqueeze(2).to_broadcast([n, TOPK, TOPK]),
                                                  v[:, h, 1, :].unsqueeze(1).to_broadcast([n, TOPK, TOPK]), ALU.add))
                nc.vector.tensor_copy(sif[r, :, :], si[r, :, :]).then_inc(s_routed_in, 1)

            def split_places():
                c.settle()
                nc.vector.tensor_copy(top_s[r, bass.ts(s, 2 * TOPK)], tv[r, :, :].rearrange("p a b -> p (a b)"))
                c.did(nc.vector.tensor_scalar(ta[r, :, :], tpos[r, :, :], 4, None, ALU.logical_shift_right))
                c.did(nc.vector.tensor_scalar(tb[r, :, :], tpos[r, :, :], TOPK - 1, None, ALU.bitwise_and))
                c.settle()
                for src, hot in ((ta, cand4), (tb, work4)):
                    for h in range(2):
                        e.did(nc.vector.tensor_tensor(hot[:, h], src[r, h, :].unsqueeze(2).to_broadcast([n, TOPK, TOPK]),
                                                      iota16[r, :].unsqueeze(1).to_broadcast([n, TOPK, TOPK]), ALU.is_equal))

            def look_up():
                e.settle()
                dve.wait_ge(s_routed_in, piece + 1)
                for a_, hot in ((0, cand4), (1, work4)):
                    for h in range(2):
                        e.did(nc.vector.tensor_tensor(hot[:, h], hot[:, h],
                                                      sif[r, 2 * h + a_, :].unsqueeze(1).to_broadcast([n, TOPK, TOPK]), ALU.mult))

            def add_up():
                e.settle()
                nc.vector.tensor_reduce(ia[r, :, :], cand4, AX.X, ALU.add)
                c.did(nc.vector.tensor_reduce(ib[r, :, :], work4, AX.X, ALU.add))

            def number():
                c.settle()
                nc.vector.scalar_tensor_tensor(out=top_i[r, bass.ts(s, 2 * TOPK)], in0=ia[r, :, :].rearrange("p a b -> p (a b)"),
                                               scalar=float(NKEYS), in1=ib[r, :, :].rearrange("p a b -> p (a b)"),
                                               op0=ALU.mult, op1=ALU.add).then_inc(s_routed, 1)
                dve.wait_ge(s_routed, piece + 2)
                assert c.n == TOPK_STEPS and e.n == 8, c.n

            return [lists_best, lists_numbers, lambda: next8(sv, works), lambda: next_numbers8(sv, si, works), sums,
                    lambda: best8(tv, cands), lambda: numbers8(tv, tpos, cands, cworks), lambda: next8(tv, cworks),
                    lambda: next_numbers8(tv, tpos, cworks), split_places, look_up, add_up, number]
        TOPK_STAGES = 13

        def logits_vector(dve, job, n):
            r = slice(0, n)
            dve.wait_ge(s_routed, PAIRS * (job + 1) + 1)
            t3 = top_s[r, :].rearrange("p (h k) -> p h k", k=TOPK)
            s3 = soft[r, :].rearrange("p (h k) -> p h k", k=TOPK)
            nc.vector.tensor_tensor(s3, t3, t3[:, :, 0:1].to_broadcast([n, HEADS, TOPK]), ALU.subtract).then_inc(s_exp_in, 1)

        def gates_vector(dve, job, n):
            r = slice(0, n)
            s3 = soft[r, :].rearrange("p (h k) -> p h k", k=TOPK)
            dve.wait_ge(s_exp, job + 1)
            c = Steps(dve, s_tail, GATE_STEPS * job)
            c.did(nc.vector.tensor_reduce(soft_sum[r, :], s3, AX.X, ALU.add))
            c.settle()
            c.did(nc.vector.reciprocal(soft_r[r, :], soft_sum[r, :]))
            c.settle()
            nc.vector.tensor_tensor(s3, s3, soft_r[r, :].unsqueeze(2).to_broadcast([n, HEADS, TOPK]), ALU.mult).then_inc(s_gate, 1)

        def tables_vector(dve, job, n, col, layer):
            dve.wait_ge(s_gateT, job + 1)
            nc.vector.tensor_copy(gateT[:, bass.ds(col, n)], FB[:, 0:n])
            nc.vector.tensor_scalar(idxT[:, bass.ds(col, n)], FB[:, P:P + n], float(EXPERTS * layer), None,
                                    ALU.add).then_inc(s_idx, 1)

        def tail_scalar(act, job, n):
            act.wait_ge(s_exp_in, job + 1)
            nc.scalar.activation(soft[0:n, :], soft[0:n, :], ACT.Exp).then_inc(s_exp, 1)

        def tail_tensor(pe, job, n):
            pe.wait_ge(s_gate, job + 1)
            apart(pe)
            nc.tensor.transpose(FB[:, 0:n], soft[0:n, :], ident[0:n, 0:n])
            nc.tensor.transpose(FB[:, P:P + n], top_i[0:n, :], ident[0:n, 0:n]).then_inc(s_gateT, 1)

        def pool_norm_scalar(act, k, jobs, n, src):
            act.wait_ge(s_yadd, k + 1)
            act.wait_ge(s_parts, jobs)
            act.wait_ge(s_saved, 16 * PARTS * jobs)
            apart(act)
            nc.scalar.activation(part[0][0:n, :], src, ACT.Square, accum_out=ss[0:n, 0:1]).then_inc(s_psq, 1)
            act.wait_ge(s_psq, 2 * k + 1)
            nc.scalar.activation(rstd[0:n, 0:1], ss[0:n, 0:1], ACT.Ln, scale=1.0 / D, bias=eps_col[0:n, :]).then_inc(s_psq, 1)
            act.wait_ge(s_psq, 2 * k + 2)
            nc.scalar.activation(rstd[0:n, 0:1], rstd[0:n, 0:1], ACT.Exp, scale=-0.5).then_inc(s_pguess, 1)

        def pool_norm_vector(dve, k, n, src):
            dve.wait_ge(s_oddw, ODD_LOADS)
            if not (isinstance(k, int) and k == 0):
                dve.wait_ge(s_prev_meta, 16)
            dve.wait_ge(s_pguess, k + 1)
            newton(dve, Steps(dve, s_pool, POOL_STEPS * k), rstd[0:n, 0:1], ss[0:n, 0:1], D, rstd[0:n, 0:1], s_pool)
            dve.wait_ge(s_pool, POOL_STEPS * (k + 1))
            nc.vector.scalar_tensor_tensor(out=hb[0:n, :], in0=src, scalar=rstd[0:n, 0:1], in1=odd_g[0:n, :],
                                           op0=ALU.mult, op1=ALU.mult).then_inc(s_hf, 1)

        def meta_prev_sync(sp_):
            sp_.wait_ge(s_hf, 1)
            sp_.wait_ge(s_setup, SETUP_STEPS)
            sp_.dma_start(prev[P - META:P, :], hb[0:META, :]).then_inc(s_prev_meta, 16)
        s_prev_meta = sem("meta_rows_placed")

        def pool_diff_tensor(pe, k, job):
            pe.wait_ge(s_hf, k + 1)
            pe.wait_ge(s_prev_meta, 16)
            pe.wait_ge(s_oddw, ODD_LOADS)
            pe.wait_ge(s_setup, SETUP_STEPS)
            pe.wait_ge(s_routed, PAIRS * job + 1)
            pe.wait_ge(s_idx, job)
            pe.wait_ge(s_keys, 8)
            for c in range(KD):
                dst = (FA, FB)[c // 4][:, P * (c % 4):P * (c % 4) + P]
                nc.tensor.matmul(dst, hb[:, P * c:P * c + P], band[:, c // 2, :], start=True, stop=False)
                last = nc.tensor.matmul(dst, prev[:, P * c:P * c + P], band_prev[:, c // 2, :], start=False, stop=True)
            last.then_inc(s_dT_ps, 1)

        def pool_mix_tensor(pe, k):
            pe.wait_ge(s_dT, 2 * k)
            for g in range(4):
                for c in range(2):
                    last = nc.tensor.matmul((FA, FB)[g // 2][:, 256 * (g % 2):256 * (g % 2) + 256], hbT[:, 2 * g + c, :],
                                            pool_w[:, g, c, :], start=(c == 0), stop=(c == 1))
            last.then_inc(s_py, 1)

        def pool_scalar(act, k):
            act.wait_ge(s_dT_ps, k)
            for half in range(2):
                nc.scalar.copy(hbT[:, 4 * half:4 * half + 4, :],
                               (FA, FB)[half].rearrange("p (k n) -> p k n", k=4)).then_inc(s_dT, 1)
            nc.scalar.copy(prev[:, :], hb[:, :]).then_inc(s_prev, 1)

        def pool_vector(dve, k, dst):
            dve.wait_ge(s_py, k)
            dve.wait_ge(s_prev, k)
            for half in range(2):
                c = slice(512 * half, 512 * half + 512)
                nc.vector.tensor_tensor(hb[:, c], (FA, FB)[half], pool_s[:, c], ALU.mult).then_inc(s_pmul, 1)
            dve.wait_ge(s_pmul, 2 * k)
            nc.vector.tensor_tensor(dst, dst, hb[:, :], ALU.add).then_inc(s_padd, 1)
            dve.wait_ge(s_padd, k)
        s_pmul = sem("pool_scaled")

        u_rows = peer_u.rearrange("l e d -> (l e) d")
        v_rows = peer_v.rearrange("l e d -> (l e) d")

        def gather_pool(pool, u, v, par):
            if u is not None:
                pool.wait_ge(s_idx_u, u + 1)
            if v is not None:
                pool.wait_ge(s_idx_v, v + 1)
            for i in range(CHUNK):
                if u is not None:
                    wait(pool, s_dot, CHUNK * u + i + 1 - U_SLOTS)
                if v is not None:
                    wait(pool, s_acc, CHUNK * v + i + 1 - V_SLOTS)
                apart(pool)
                if u is not None:
                    nc.gpsimd.indirect_dma_start(u_ring[:, i % U_SLOTS, :], None, u_rows,
                                                 bass.IndirectOffsetOnAxis(idx_u[par][:, i:i + 1], 0)
                                                 ).then_inc(s_u[i % U_SLOTS], 16)
                if v is not None:
                    nc.gpsimd.indirect_dma_start(v_ring[:, i % V_SLOTS, :], None, v_rows,
                                                 bass.IndirectOffsetOnAxis(idx_v[par][:, i:i + 1], 0)
                                                 ).then_inc(s_v[i % V_SLOTS], 16)

        def at_token(hooks, i):
            for at, step in hooks:
                if at == i:
                    step()

        def experts_tensor(pe, u, v, par, fetched, hooks=()):
            if u is not None:
                pe.wait_ge(s_fetched[par], 16 * fetched)
            for i in range(CHUNK):
                if u is not None:
                    wait(pe, s_dot, CHUNK * u + i - 1)
                    for half in range(2):
                        ins = nc.tensor.matmul(bc[i % 2][:, half, :], pick[:, i, :],
                                               hparts[:, par, 512 * half:512 * half + 512], start=True, stop=True)
                    ins.then_inc(s_bc, 1)
                if v is not None:
                    pe.wait_ge(s_v[i % V_SLOTS], 16 * ((CHUNK // V_SLOTS) * v + i // V_SLOTS + 1))
                    pe.wait_ge(s_wcol, CHUNK * v + i + 1)
                    for half in range(2):
                        ins = nc.tensor.matmul(y_ps[:, half, :], w_col[:, i % W_SLOTS, :],
                                               v_ring[:, i % V_SLOTS, 512 * half:512 * half + 512],
                                               start=False, stop=False, skip_group_check=True)
                    ins.then_inc(s_acc, 1)
                at_token(hooks, i)

        def open_sum(pe, tiles):
            wait(pe, s_yadd, tiles)
            pe.wait_ge(s_setup, SETUP_STEPS)
            for half in range(2):
                nc.tensor.matmul(y_ps[:, half, :], zeros[:, 0:P], zeros[:, :], start=True, stop=False, skip_group_check=True)

        def close_sum(pe):
            for half in range(2):
                ins = nc.tensor.matmul(y_ps[:, half, :], zeros[:, 0:P], zeros[:, :], start=False, stop=True, skip_group_check=True)
            ins.then_inc(s_y, 1)

        def stage_u(act, u, par):
            wait(act, s_dot, CHUNK * (u - 1))
            apart(act)
            nc.scalar.copy(idx_u[par][:, :], idxT[:, bass.ds(CHUNK * u, CHUNK)]).then_inc(s_idx_u, 1)

        def stage_v(act, v, par):
            wait(act, s_acc, CHUNK * (v - 1))
            apart(act)
            nc.scalar.copy(idx_v[par][:, :], idxT[:, bass.ds(CHUNK * v, CHUNK)]).then_inc(s_idx_v, 1)

        def gelu_scalar(act, u):
            act.wait_ge(s_garg, u + 1)
            wait(act, s_weight, u)
            nc.scalar.activation(ge[:, :], ga[:, :], ACT.Exp, scale=-1.0).then_inc(s_gexp, 1)

        def columns_scalar(act, v, par, pos, hooks=()):
            act.wait_ge(s_weight, v + 1)
            for i in range(CHUNK):
                wait(act, s_acc, CHUNK * v + i + 1 - W_SLOTS)
                nc.scalar.activation(w_col[:, i % W_SLOTS, :], strip[:, bass.ds(P - 1 - i - pos, P)], ACT.Copy,
                                     scale=weight[par][:, i:i + 1]).then_inc(s_wcol, 1)
                at_token(hooks, i)

        def gelu_argument(dve, u, par):
            c = Steps(dve, s_gelu, (GELU1 + GELU2) * u)
            dve.wait_ge(s_dot, CHUNK * (u + 1))
            if not (isinstance(u, int) and u == 0):
                dve.wait_ge(s_gexp, u)
            c.did(nc.vector.tensor_tensor(ga[:, :], dot[par][:, :], dot[par][:, :], ALU.mult))
            c.settle()
            c.did(nc.vector.tensor_scalar(ga[:, :], ga[:, :], GELU_B, GELU_A, ALU.mult, ALU.add))
            c.settle()
            c.did(nc.vector.tensor_tensor(ga[:, :], ga[:, :], dot[par][:, :], ALU.mult))
            c.settle()
            nc.vector.tensor_scalar(ga[:, :], ga[:, :], -80.0, None, ALU.max).then_inc(s_garg, 1)

        def gelu_weights(dve, u, par):
            c = Steps(dve, s_gelu, (GELU1 + GELU2) * u + GELU1)
            wait(dve, s_weight, u)
            c.did(nc.vector.tensor_tensor(gx[:, :], dot[par][:, :], gateT[:, bass.ds(CHUNK * u, CHUNK)], ALU.mult))
            dve.wait_ge(s_gexp, u + 1)
            c.did(nc.vector.tensor_scalar(ge[:, :], ge[:, :], 1.0, None, ALU.add))
            c.settle()
            c.did(nc.vector.reciprocal(ge[:, :], ge[:, :]))
            c.settle()
            wait(dve, s_wcol, CHUNK * (u - 1))
            nc.vector.tensor_tensor(weight[par][:, :], gx[:, :], ge[:, :], ALU.mult).then_inc(s_weight, 1)

        def dots_vector(dve, u, par, hooks=(), first=False):
            for i in range(CHUNK):
                dve.wait_ge(s_u[i % U_SLOTS], 16 * ((CHUNK // U_SLOTS) * u + i // U_SLOTS + 1))
                dve.wait_ge(s_bc, CHUNK * u + i + 1)
                row = u_ring[:, i % U_SLOTS, :]
                nc.vector.scalar_tensor_tensor(out=row, in0=row, scalar=1.0, in1=bc[i % 2].rearrange("p a b -> p (a b)"),
                                               op0=ALU.mult, op1=ALU.mult, accum_out=dot[par][:, i:i + 1]).then_inc(s_dot, 1)
                if i == 3 and not first:
                    gelu_weights(dve, u - 1, 1 - par)
                at_token(hooks, i)
            gelu_argument(dve, u, par)

        def take_sum(dve, tiles, dst, n):
            dve.wait_ge(s_y, tiles + 1)
            nc.vector.tensor_tensor(dst, dst, y_ps[0:n, :, :].rearrange("p a b -> p (a b)"), ALU.add).then_inc(s_yadd, 1)
            dve.wait_ge(s_yadd, tiles + 1)

        def tile_of(slot, n=P):
            return hres[0:n, bass.ds(slot, 1), :].rearrange("p a d -> p (a d)")

        META_ROWS = hres[0:META, XT, :]
        LAST = 2 * XT - 1
        QUERY_BANK = psum[:, 0, :]

        def routing_tensor(pe, job, s):
            p0 = PAIRS * job + 2 * s

            def query(e, k):
                def step():
                    if k == 0:
                        pe.wait_ge(s_read, p0 + e)
                        pe.wait_ge(s_hbT, 2 * job + 2)
                    query_tensor(pe, p0 + e, 2 * s + e, P, k, k + 2, FA)
                return step
            first = [(0, query(0, 0)), (1, query(0, 2)), (3, query(0, 4)), (4, query(0, 6)),
                     (6, lambda: queryT_tensor(pe, p0, P)), (8, lambda: scores_tensor(pe, p0, 2 * s, P)),
                     (11, query(1, 0)), (12, query(1, 2)), (13, query(1, 4)), (14, query(1, 6))]
            second = [(0, lambda: queryT_tensor(pe, p0 + 1, P)), (2, lambda: scores_tensor(pe, p0 + 1, 2 * s + 1, P))]
            return first, second

        def routing_scalar(act, job, s):
            p0 = PAIRS * job + 2 * s
            first = [(5, lambda: query_scalar(act, p0, P, FA)), (7, lambda: queryT_scalar(act, p0, P)),
                     (15, lambda: query_scalar(act, p0 + 1, P, FA))]
            second = [(1, lambda: queryT_scalar(act, p0 + 1, P))]
            return first, second

        def routing_vector(dve, job, s):
            p0 = PAIRS * job + 2 * s
            a = topk_stages(dve, p0, 2 * s, P)
            b = topk_stages(dve, p0 + 1, 2 * s + 1, P)
            first = [(9 + i, a[i]) for i in range(7)]
            second = [(min(i, 4), a[7 + i]) for i in range(6)] + [(min(5 + i, 15), b[i]) for i in range(TOPK_STAGES)]
            return first, second

        def start_stages_tensor(pe, job, k):
            layer = 0 if k is None else 1
            pooling = [] if k is None else [(2, lambda: pool_diff_tensor(pe, k, job)), (5, lambda: pool_mix_tensor(pe, k))]
            return pooling + [(3 if k is None else 11, lambda: start_tensor(pe, job, P, layer))]

        def start_stages_scalar(act, job, k, src):
            def norm():
                if k is not None:
                    act.wait_ge(s_padd, k)
                norm_scalar(act, job, P, src)
            if k is None:
                return [(0, norm), (4, lambda: transposed_scalar(act, job, P))]
            return [(0, lambda: pool_norm_scalar(act, k, job, P, src)), (3, lambda: pool_scalar(act, k)), (9, norm),
                    (12, lambda: transposed_scalar(act, job, P))]

        def start_stages_vector(dve, job, k, src):
            at = 1 if k is None else 10
            pooling = [] if k is None else [(1, lambda: pool_norm_vector(dve, k, P, src)), (7, lambda: pool_vector(dve, k, src))]

            def split(i):
                return lambda: split_vector(dve, job, P, i)
            return pooling + [(at, lambda: norm_vector(dve, job, P, src, 0 if k is None else 1))] + \
                [(min(at + 2 + i, 15), split(i)) for i in range(SPLIT + 1)]

        block = ctx.enter_context(nc.Block())

        @block.sync
        def _(sp_):
            mixer_sync(sp_)
            wq_sync(sp_, 0, 0, WQ_EARLY)
            wq_sync(sp_, 0, WQ_EARLY, KD)
            keys_sync(sp_, 0, 0)
            keys_sync(sp_, 0, 1)
            odd_weights_sync(sp_)
            save_parts(sp_, 0, 0, META)
            save_parts(sp_, 1, 1, P)
            for u in range(4):
                fetch_parts(sp_, u, u % 2)
            save_parts(sp_, 2, 1 + TILE_CHUNKS, P)
            meta_prev_sync(sp_)

            def chunk_of(j, s):
                return TILE_CHUNKS * j + 3 + 2 * s

            def pair(j, s):
                fetch_parts(sp_, chunk_of(j, s) + 1, 0)
                fetch_parts(sp_, chunk_of(j, s) + 2, 1)

            def save(j):
                save_parts(sp_, j + 3, TILE_CHUNKS * (j + 2) + 1, P)

            with sp_.Fori(0, 2) as j:
                with sp_.Fori(0, PAIRS) as s:
                    pair(j, s)
                save(j)
            with sp_.Fori(0, 2) as s:
                pair(2, s)
            keys_sync(sp_, 1, 0)
            wq_sync(sp_, 1, 0, 2)
            fetch_parts(sp_, chunk_of(2, 2) + 1, 0)
            wq_sync(sp_, 1, 2, 5)
            fetch_parts(sp_, chunk_of(2, 2) + 2, 1)
            keys_sync(sp_, 1, 1)
            wq_sync(sp_, 1, 5, KD)
            fetch_parts(sp_, chunk_of(2, 3) + 1, 0)
            fetch_parts(sp_, chunk_of(2, 3) + 2, 1)
            save(2)
            with sp_.Fori(3, 6) as j:
                with sp_.Fori(0, PAIRS) as s:
                    pair(j, s)
                save(j)
            with sp_.Fori(0, PAIRS) as s:
                pair(LAST - 1, s)
            with sp_.Fori(0, PAIRS - 2) as s:
                pair(LAST, s)
            fetch_parts(sp_, CHUNKS - 1, 0)
            sp_.wait_ge(s_yadd, 2 + LAST)
            sp_.dma_start(out[0].rearrange("(t p) d -> p t d", p=P), hres[:, 0:XT, :]).then_inc(s_out, 16)
            sp_.wait_ge(s_out, 16)

        @block.gpsimd
        def _(pool):
            n = mixer_constants(pool)
            assert n == MIXER_CONSTANTS
            expert_constants(pool)
            gather_pool(pool, 0, None, 0)
            gather_pool(pool, 1, None, 1)
            gather_pool(pool, 2, 0, 0)

            def pair(j, s):
                u = TILE_CHUNKS * j + 3 + 2 * s
                gather_pool(pool, u, u - 2, 1)
                gather_pool(pool, u + 1, u - 1, 0)

            with pool.Fori(0, LAST) as j:
                with pool.Fori(0, PAIRS) as s:
                    pair(j, s)
            with pool.Fori(0, PAIRS - 1) as s:
                pair(LAST, s)
            gather_pool(pool, None, CHUNKS - 2, 1)
            gather_pool(pool, None, CHUNKS - 1, 0)

        @block.scalar
        def _(act):
            mixer_scalar(act)
            act.wait_ge(s_mix, 2 * TILES)
            keys_scalar(act, 0, 0)
            keys_scalar(act, 0, 1)

            def route(job, n, src):
                norm_scalar(act, job, n, src)
                transposed_scalar(act, job, n)
                with act.Fori(0, PAIRS) as s:
                    query_scalar(act, PAIRS * job + s, n, QUERY_BANK)
                    queryT_scalar(act, PAIRS * job + s, n)
                tail_scalar(act, job, n)

            def pair(j, s, first=(), second=(), stage_last=True):
                u = TILE_CHUNKS * j + 3 + 2 * s
                stage_u(act, u + 1, 0)
                stage_v(act, u - 1, 0)
                gelu_scalar(act, u - 1)
                columns_scalar(act, u - 2, 1, 2 * CHUNK * s, first)
                if stage_last:
                    stage_u(act, u + 2, 1)
                stage_v(act, u, 1)
                gelu_scalar(act, u)
                columns_scalar(act, u - 1, 0, 2 * CHUNK * s + CHUNK, second)

            def iteration(j, start=(), keys=()):
                with act.Fori(0, 2) as s:
                    pair(j, s, *routing_scalar(act, j + 2, s))
                pair(j, 2, [(1, lambda: tail_scalar(act, j + 2, P))], keys)
                act.wait_ge(s_idx, j + 3)
                pair(j, 3, start)

            route(0, META, META_ROWS)
            route(1, P, tile_of(0))
            act.wait_ge(s_idx, 2)
            stage_u(act, 0, 0)
            stage_u(act, 1, 1)
            norm_scalar(act, 2, P, tile_of(1))
            stage_u(act, 2, 0)
            stage_v(act, 0, 0)
            transposed_scalar(act, 2, P)
            gelu_scalar(act, 0)
            stage_u(act, 3, 1)
            stage_v(act, 1, 1)
            gelu_scalar(act, 1)
            act.wait_ge(s_setup, SETUP_STEPS)
            columns_scalar(act, 0, 0, 0)
            pool_norm_scalar(act, 0, 3, META, META_ROWS)

            with act.Fori(0, 2) as j:
                iteration(j, start_stages_scalar(act, j + 3, None, tile_of(j + 2)))
            iteration(2, start_stages_scalar(act, 5, 1, tile_of(0)),
                      [(4, lambda: keys_scalar(act, 1, 0)), (11, lambda: keys_scalar(act, 1, 1))])
            with act.Fori(3, 6) as j:
                iteration(j, start_stages_scalar(act, j + 3, j - 1, tile_of(j - 2)))
            iteration(LAST - 1)
            with act.Fori(0, PAIRS - 2) as s:
                pair(LAST, s)
            pair(LAST, PAIRS - 2, stage_last=False)
            stage_v(act, CHUNKS - 1, 0)
            gelu_scalar(act, CHUNKS - 1)
            columns_scalar(act, CHUNKS - 2, 1, 2 * CHUNK * (PAIRS - 1))
            columns_scalar(act, CHUNKS - 1, 0, 2 * CHUNK * (PAIRS - 1) + CHUNK)

        @block.vector
        def _(dve):
            mixer_vector(dve)
            dve.wait_ge(s_mix, 2 * TILES)
            dve.wait_ge(s_setup, SETUP_STEPS)
            nc.vector.memset(tv[:, :, :], 0.0).then_inc(s_routed, 1)
            dve.wait_ge(s_routed, 1)

            def route(job, n, src, col):
                norm_vector(dve, job, n, src, 0)
                for i in range(SPLIT + 1):
                    split_vector(dve, job, n, i)
                with dve.Fori(0, PAIRS) as s:
                    for stage in topk_stages(dve, PAIRS * job + s, s, n):
                        stage()
                logits_vector(dve, job, n)
                gates_vector(dve, job, n)
                tables_vector(dve, job, n, col, 0)

            def pair(j, s, first=(), second=()):
                u = TILE_CHUNKS * j + 3 + 2 * s
                dots_vector(dve, u, 1, first)
                dots_vector(dve, u + 1, 0, second)

            def iteration(j, layer, start=()):
                job = j + 2
                with dve.Fori(0, 2) as s:
                    pair(j, s, *routing_vector(dve, job, s))
                pair(j, 2, [(0, lambda: logits_vector(dve, job, P)), (2, lambda: gates_vector(dve, job, P)),
                            (4, lambda: tables_vector(dve, job, P, META + P * (j + 1), layer))])
                pair(j, 3, start)
                take_sum(dve, j + 1, tile_of(j % XT), P)

            route(0, META, META_ROWS, 0)
            route(1, P, tile_of(0), META)
            dots_vector(dve, 0, 0, first=True)
            norm_vector(dve, 2, P, tile_of(1), 0)
            dots_vector(dve, 1, 1, [(2 + i, lambda i=i: split_vector(dve, 2, P, i)) for i in range(SPLIT + 1)])
            dots_vector(dve, 2, 0)
            take_sum(dve, 0, META_ROWS, META)
            pool_norm_vector(dve, 0, META, META_ROWS)

            with dve.Fori(0, 2) as j:
                iteration(j, 0, start_stages_vector(dve, j + 3, None, tile_of(j + 2)))
            iteration(2, 0, start_stages_vector(dve, 5, 1, tile_of(0)))
            with dve.Fori(3, 6) as j:
                iteration(j, 1, start_stages_vector(dve, j + 3, j - 1, tile_of(j - 2)))
            iteration(LAST - 1, 1)
            with dve.Fori(0, PAIRS - 1) as s:
                pair(LAST, s)
            gelu_weights(dve, CHUNKS - 1, 0)
            take_sum(dve, LAST + 1, tile_of(XT - 1), P)

        @block.tensor
        def _(pe):
            mixer_tensor(pe)
            pe.wait_ge(s_mix, 2 * TILES)
            keys_tensor(pe, 0, 0)
            keys_tensor(pe, 0, 1)

            def route(job, n):
                start_tensor(pe, job, n, 0)
                pe.wait_ge(s_hbT, 2 * job + 2)
                query_tensor(pe, PAIRS * job, 0, n, 0, KD, QUERY_BANK)

                def piece(s, more):
                    queryT_tensor(pe, PAIRS * job + s, n)
                    if not (job == 0 and isinstance(s, int) and s == 0):
                        pe.wait_ge(s_read, PAIRS * job + s)
                    scores_tensor(pe, PAIRS * job + s, s, n)
                    if more:
                        query_tensor(pe, PAIRS * job + s + 1, s + 1, n, 0, KD, QUERY_BANK)
                piece(0, True)
                with pe.Fori(1, PAIRS - 1) as s:
                    piece(s, True)
                piece(PAIRS - 1, False)
                tail_tensor(pe, job, n)

            def pair(j, s, first=(), second=()):
                u = TILE_CHUNKS * j + 3 + 2 * s
                fetched = PAIRS * j + 1 + s
                experts_tensor(pe, u, u - 2, 1, fetched + 1, first)
                experts_tensor(pe, u + 1, u - 1, 0, fetched + 2, second)

            def iteration(j, start=(), keys=()):
                open_sum(pe, j + 1)
                with pe.Fori(0, 2) as s:
                    pair(j, s, *routing_tensor(pe, j + 2, s))
                pair(j, 2, [(3, lambda: tail_tensor(pe, j + 2, P))], keys)
                pair(j, 3, start)
                close_sum(pe)

            pe.wait_ge(s_setup, SETUP_STEPS)
            route(0, META)
            route(1, P)
            experts_tensor(pe, 0, None, 0, 1)
            start_tensor(pe, 2, P, 0)
            experts_tensor(pe, 1, None, 1, 1)
            open_sum(pe, 0)
            experts_tensor(pe, 2, 0, 0, 2)
            close_sum(pe)
            with pe.Fori(0, 2) as j:
                iteration(j, start_stages_tensor(pe, j + 3, None))
            iteration(2, start_stages_tensor(pe, 5, 1),
                      [(2, lambda: keys_tensor(pe, 1, 0)), (9, lambda: keys_tensor(pe, 1, 1))])
            with pe.Fori(3, 6) as j:
                iteration(j, start_stages_tensor(pe, j + 3, j - 1))
            iteration(LAST - 1)
            open_sum(pe, LAST + 1)
            with pe.Fori(0, PAIRS - 1) as s:
                pair(LAST, s)
            experts_tensor(pe, None, CHUNKS - 2, 1, 0)
            experts_tensor(pe, None, CHUNKS - 1, 0, 0)
            close_sum(pe)


_INS = ["x", "meta_tokens", "even_norm_g", "even_w_in", "even_q_norm_g", "even_k_norm_g", "even_conv_w", "even_w_out",
        "odd_norm_g", "odd_pool_w", "odd_pool_scale", "ffn_norm_g", "peer_w_query", "peer_sub_keys", "peer_u", "peer_v"]


def kernel(**inputs):
    import concourse.bacc as bacc
    from concourse.bass_utils import run_bass_kernel_spmd

    nc = bacc.Bacc("TRN2", target_bir_lowering=False, num_devices=1)
    arrays, args = {}, []
    for name in _INS:
        a = np.ascontiguousarray(inputs[name])
        arrays[f"in_{name}"] = a
        args.append(nc.dram_tensor(f"in_{name}", a.shape, mybir.dt.from_np(a.dtype), kind="ExternalInput").ap())
    out = nc.dram_tensor("out", (1, SEQ, D), F32, kind="ExternalOutput").ap()
    program(nc, *args, out)
    r = run_bass_kernel_spmd(nc, [arrays], core_ids=[0])
    return r.results[0]["out"]
```

```python
import numpy as np
import concourse.bass as bass
from concourse import mybir
from contextlib import ExitStack

F32 = mybir.dt.float32
BF16 = mybir.dt.bfloat16
U32 = mybir.dt.uint32
ALU = mybir.AluOpType
ACT = mybir.ActivationFunctionType
AX = mybir.AxisListType

P = 128
D = 1024
KD = D // P
META = 16
SEQ = 512
XT = SEQ // P
TILES = XT + 1
HEADS = 8
DH = 64
CONV = 512
GROUP = 512
EPS = 1e-6
NKEYS = 128
TOPK = 16
EXPERTS = NKEYS * NKEYS
CHUNK = 16
TILE_CHUNKS = P // CHUNK
PAIRS = TILE_CHUNKS // 2
CHUNKS = 1 + 2 * XT * TILE_CHUNKS
U_SLOTS = 4
V_SLOTS = 4
W_SLOTS = 4
LISTS = 4
WINDOWS = (2, 4, 8, 16)
PARTS = 3
BIG = 1e30
GELU_A = 2 * 0.7978845608028654
GELU_B = GELU_A * 0.044715


class Steps:

    def __init__(self, eng, sem, base=0):
        self.eng, self.sem, self.base, self.n = eng, sem, base, 0

    def did(self, ins):
        ins.then_inc(self.sem, 1)
        self.n += 1

    def settle(self):
        self.eng.wait_ge(self.sem, self.base + self.n)


def wait(eng, sem, value):
    if not (isinstance(value, int) and value <= 0):
        eng.wait_ge(sem, value)


def apart(eng):
    eng.nop(nofuse=True)


def first_piece(job):
    return 0 if isinstance(job, int) and job == 0 else PAIRS * job - (PAIRS - 1)


def rows_of(tile):
    return META if tile == XT else P


def cols_of(tile):
    return slice(SEQ, SEQ + META) if tile == XT else slice(P * tile, P * tile + P)


def program(nc, x, meta_tokens, even_norm_g, even_w_in, even_q_norm_g, even_k_norm_g, even_conv_w,
            even_w_out, odd_norm_g, odd_pool_w, odd_pool_scale, ffn_norm_g, peer_w_query,
            peer_sub_keys, peer_u, peer_v, out):
    ctx = ExitStack()
    mixer = ExitStack()
    with ctx:
        def sem(name):
            return ctx.enter_context(nc.semaphore(name))

        def sb(name, shape, dt=F32, where=ctx):
            return where.enter_context(nc.sbuf_tensor(name, shape, dt))

        hres = sb("hres", [P, TILES, D])
        ident = sb("ident", [P, P])
        eps_col = sb("eps_col", [P, 1])
        ss = sb("ss", [P, TILES])
        rstd = sb("rstd", [P, TILES])
        nt_a = sb("newton_a", [P, 80])
        nt_b = sb("newton_b", [P, 80])
        psum = ctx.enter_context(nc.psum_tensor("psum", [P, 8, 512], F32))

        with mixer:
            def sbm(name, shape, dt=F32):
                return sb(name, shape, dt, mixer)
            hT = sbm("hT", [P, KD, SEQ + META])
            xn = sbm("xn", [P, 2, D])
            gate_b = sbm("gate_b", [P, 4, META + SEQ])
            conv_in = sbm("conv_in", [P, 4, 2 + META + SEQ])
            conv_y = sbm("conv_y", [P, META + SEQ])
            qkv = sbm("qkv", [P, TILES, 3, GROUP])
            w_ring = sbm("w_ring", [P, 2, KD, GROUP])
            catT = sbm("catT", [P, KD, SEQ + META])
            qs = [sbm(f"qs{i}", [P, TILES, DH]) for i in range(2)]
            ks = [sbm(f"ks{i}", [P, TILES, DH]) for i in range(2)]
            vs = [sbm(f"vs{i}", [P, TILES, DH]) for i in range(2)]
            qT = [sbm(f"qT{i}", [DH, SEQ + META]) for i in range(2)]
            kT = [sbm(f"kT{i}", [DH, SEQ + P]) for i in range(2)]
            sp = [sbm(f"softplus{i}", [P, 4, 512]) for i in range(2)]
            wts = sbm("wts", [P, 4, 512])
            ssqk = sbm("ssqk", [P, TILES, 16])
            rqk = sbm("rqk", [P, TILES, 16])
            even_g = sbm("even_g", [P, KD])
            qg = sbm("qg", [DH, 1])
            qg8 = sbm("qg8", [DH, 1])
            kg = sbm("kg", [DH, 1])
            conv_w = sbm("conv_w", [P, 3, 4])
            causal = sbm("causal", [P, P])
            neg = sbm("neg", [P, P], BF16)
            ident_b = sbm("ident_bf16", [P, P], BF16)
            neg_rest = sbm("neg_rest", [P, P])
            neg_tri = sbm("neg_tri", [P, P])
            neg_ones = sbm("neg_ones", [P, P])
            w_out_sb = w_ring[:, :, :, :].rearrange("p a k n -> p (a k n)").rearrange("p (k n) -> p k n", k=KD)

        wq = sb("wq", [P, KD, 2 * D])
        WQ_EARLY = 5
        keysT = sb("keysT", [P, 2 * HEADS, NKEYS])
        u_ring = sb("u_ring", [P, U_SLOTS, D])
        v_ring = sb("v_ring", [P, V_SLOTS, D])
        hparts = sb("hparts", [PARTS * CHUNK, 2, D], BF16)
        odd_g = sb("odd_g", [P, D])
        pool_s = sb("pool_s", [P, D])
        w_col = sb("w_col", [P, W_SLOTS, P])
        pool_w = sb("pool_w", [P, 4, 2, 256])
        hb = sb("hb", [P, D])
        hbT = sb("hbT", [P, KD, P])
        part = [sb(f"part{i}", [P, D], BF16) for i in range(PARTS)]
        pick = sb("pick", [PARTS * CHUNK, CHUNK, P], BF16)
        ffn_g = sb("ffn_g", [P, D])
        prev = sb("prev", [P, D])
        band = sb("band", [P, 4, P])
        band_prev = sb("band_prev", [P, 4, P])
        q_sb = sb("q_sb", [P, 512])
        q_T = sb("q_T", [P, LISTS, P])
        work = sb("work", [P, 512])
        cand = sb("cand", [P, 512])
        sv = sb("sv", [P, LISTS, TOPK])
        si = sb("si", [P, LISTS, TOPK], U32)
        sif = sb("sif", [P, LISTS, TOPK])
        tv = sb("tv", [P, 2, TOPK])
        tpos = sb("tpos", [P, 2, TOPK], U32)
        ta = sb("ta", [P, 2, TOPK], U32)
        tb = sb("tb", [P, 2, TOPK], U32)
        ia = sb("ia", [P, 2, TOPK])
        ib = sb("ib", [P, 2, TOPK])
        iota16 = sb("iota16", [P, TOPK])
        top_s = sb("top_s", [P, P])
        top_i = sb("top_i", [P, P])
        soft = sb("soft", [P, P])
        soft_sum = sb("soft_sum", [P, HEADS])
        soft_r = sb("soft_r", [P, HEADS])
        idxT = sb("idxT", [P, CHUNKS * CHUNK], U32)
        gateT = sb("gateT", [P, CHUNKS * CHUNK])
        idx_u = [sb(f"idx_u{i}", [P, CHUNK], U32) for i in range(2)]
        idx_v = [sb(f"idx_v{i}", [P, CHUNK], U32) for i in range(2)]
        dot = [sb(f"dot{i}", [P, CHUNK]) for i in range(2)]
        weight = [sb(f"weight{i}", [P, CHUNK]) for i in range(2)]
        ga = sb("ga", [P, CHUNK])
        meta_tables = sb("meta_tables", [P, 2 * META])
        ge = sb("ge", [P, CHUNK])
        gx = sb("gx", [P, CHUNK])
        strip = sb("strip", [P, 2 * P - 1])
        zeros = sb("zeros", [P, 512], BF16)
        parts_dram = nc.dram_tensor("parts_dram", [CHUNKS, PARTS, CHUNK, D], BF16, kind="Internal").ap()

        bc = [psum[:, 0:2, :], psum[:, 2:4, :]]
        y_ps = psum[:, 4:6, :]
        FA, FB = psum[:, 6, :], psum[:, 7, :]

        s_x = [sem(f"x_loaded{t}") for t in range(TILES)]
        s_small = sem("small_loaded")
        s_win = [sem(f"w_in_loaded{i}") for i in range(2)]
        s_wout = sem("w_out_loaded")
        s_const = sem("mixer_constants_step")
        s_setup = sem("expert_constants_step")
        s_iota = sem("place_numbers_ready")
        s_act = sem("act_step")
        s_dve = sem("dve_step")
        s_ss = sem("squares_summed")
        s_rstd = sem("rstd_ready")
        s_xn = sem("xn_ready")
        s_xnT = sem("xn_transposed")
        s_hT = sem("hT_ready")
        s_qkv_ps = sem("qkv_multiplied")
        s_qkv = sem("qkv_copied")
        s_fm_ps = sem("conv_inputs_multiplied")
        s_fm_a = sem("conv_gates_copied")
        s_fm_u = sem("conv_u_used")
        s_ssqk = sem("qk_squares_summed")
        s_rqk0 = sem("qk_rstd_guessed")
        s_rqk = sem("qk_rstd_ready")
        s_conv = sem("conv_done")
        s_qk_in = sem("head_qk_scaled")
        s_v_in = sem("head_v_copied")
        s_qkT_ps = sem("head_qk_transposed")
        s_qkT = sem("head_qkT_copied")
        s_z = sem("scores_ready")
        s_log = sem("log_terms_ready")
        s_soft = sem("softplus_step")
        s_sp = sem("softplus_ready")
        s_S = sem("log_weights_ready")
        s_w = sem("weights_ready")
        s_av = sem("head_attended")
        s_att = sem("head_copied")
        s_proj = sem("out_projected")
        s_mix = sem("mixer_added")

        s_wq = sem("w_query_loaded")
        s_keys_raw = [sem(f"keys_loaded{i}") for i in range(2)]
        s_keys_ps = sem("keys_transposed")
        s_keys = sem("keys_copied")
        s_ffng = sem("ffn_gain_loaded")
        s_oddw = sem("odd_weights_loaded")
        s_hsq = sem("h_squares_step")
        s_hguess = sem("h_rstd_guessed")
        s_hnewton = sem("h_newton_step")
        s_hb = sem("hb_ready")
        s_hbT_ps = sem("hb_transposed")
        s_hbT = sem("hbT_copied")
        s_split = sem("hb_split_step")
        s_parts = sem("hb_parts_ready")
        s_saved = sem("hb_parts_saved")
        s_fetched = [sem(f"chunk_parts_fetched{i}") for i in range(2)]
        s_q_ps = sem("query_multiplied")
        s_q = sem("query_copied")
        s_qT_ps = sem("query_transposed")
        s_qT = sem("queryT_copied")
        s_sc = sem("key_scores_ready")
        s_topk = sem("topk_step")
        s_routed = sem("two_heads_routed")
        s_tail = sem("gate_step")
        s_exp_in = sem("gate_logits_ready")
        s_exp = sem("gate_exponentials_ready")
        s_gate = sem("gates_ready")
        s_gateT = sem("gates_transposed")
        s_idx = sem("tile_routed")
        s_pool = sem("pool_step")
        s_psq = sem("pool_squares_step")
        s_pguess = sem("pool_rstd_guessed")
        s_hf = sem("pool_input_ready")
        s_dT_ps = sem("pool_differences_ready")
        s_dT = sem("pool_differences_copied")
        s_prev = sem("previous_rows_kept")
        s_py = sem("pool_multiplied")
        s_padd = sem("pool_added")

        s_idx_u = sem("u_indices_staged")
        s_idx_v = sem("v_indices_staged")
        s_u = [sem(f"u_rows_landed{i}") for i in range(U_SLOTS)]
        s_v = [sem(f"v_rows_landed{i}") for i in range(V_SLOTS)]
        s_bc = sem("token_row_broadcast")
        s_dot = sem("token_dotted")
        s_gelu = sem("gelu_step")
        s_garg = sem("gelu_argument_ready")
        s_gexp = sem("gelu_exponential_ready")
        s_weight = sem("expert_weights_ready")
        s_wcol = sem("weight_column_ready")
        s_acc = sem("token_accumulated")
        s_y = sem("tile_summed")
        s_yadd = sem("tile_added")
        s_out = sem("output_stored")

        KEY_BLOCKS = [3, 2, 1, 0]
        Z_AT = {3: (0, 0), 2: (0, P), 1: (1, 0), 0: (2, 0), XT: (3, 0)}
        Z_META = (1, 384)
        SEGMENTS = [(slice(0, 1), 0, 384), (slice(1, 2), 0, 400), (slice(2, 4), 0, 512)]

        def z_cols(t, b):
            bank, at = Z_AT[b]
            return t[:, bank, at:at + (512 if b == XT else SEQ - P * b)]

        NEWTON = 4
        SPLIT = 4
        TOPK_STEPS = 34
        GATE_STEPS = 2
        POOL_STEPS = NEWTON + 1
        GELU1, GELU2 = 3, 3

        def newton(dve, steps, guess, total, n, result, last):
            w = guess.shape[-1]
            a, b = nt_a[0:guess.shape[0], 0:w], nt_b[0:guess.shape[0], 0:w]
            steps.did(nc.vector.tensor_scalar(a, total, 1.0 / n, EPS, ALU.mult, ALU.add))
            steps.did(nc.vector.tensor_tensor(b, guess, guess, ALU.mult))
            steps.settle()
            steps.did(nc.vector.tensor_tensor(b, b, a, ALU.mult))
            steps.settle()
            steps.did(nc.vector.tensor_scalar(b, b, -0.5, 1.5, ALU.mult, ALU.add))
            steps.settle()
            nc.vector.tensor_tensor(result, guess, b, ALU.mult).then_inc(last, 1)

        META_ROWS = hres[0:META, XT, :]

        def mixer_sync(sp_):
            for t in range(XT):
                sp_.dma_start(hres[:, t, :], x[0, P * t:P * t + P, :]).then_inc(s_x[t], 16)
            sp_.dma_start(hres[0:META, XT, :], meta_tokens[:, :]).then_inc(s_x[XT], 16)
            w_in = even_w_in[0].rearrange("(k p) n -> p k n", p=P)
            for g in range(6):
                if g >= 2:
                    if g - 2 < 3:
                        sp_.wait_ge(s_qkv_ps, TILES * (g - 1))
                    else:
                        sp_.wait_ge(s_fm_ps, 4 * (g - 4))
                sp_.dma_start(w_ring[:, g % 2, :, :], w_in[:, :, GROUP * g:GROUP * g + GROUP]).then_inc(s_win[g % 2], 16)
                if g == 0:
                    sp_.dma_start(even_g[:, :], even_norm_g[0].rearrange("(k p) -> p k", p=P), allow_slow_non_contiguous=True).then_inc(s_small, 16)
                    sp_.dma_start(qg[:, :], even_q_norm_g[0].rearrange("(p a) -> p a", a=1),
                                  allow_slow_non_contiguous=True).then_inc(s_small, 16)
                    sp_.dma_start(kg[:, :], even_k_norm_g[0].rearrange("(p a) -> p a", a=1),
                                  allow_slow_non_contiguous=True).then_inc(s_small, 16)
                    for i in range(3):
                        sp_.dma_start(conv_w[:, i, :], even_conv_w[0, i].rearrange("(m p) -> p m", p=P),
                                      allow_slow_non_contiguous=True).then_inc(s_small, 16)
            sp_.wait_ge(s_fm_ps, 12)
            sp_.dma_start(w_out_sb, even_w_out[0].rearrange("(k p) n -> p k n", p=P)).then_inc(s_wout, 16)
        SMALL = 6 * 16

        def wq_sync(sp_, layer, k0, k1):
            if layer == 0:
                if k0 == 0:
                    sp_.wait_ge(s_fm_ps, 12)
                    sp_.wait_ge(s_conv, 8)
                    sp_.wait_ge(s_ssqk, TILES)
                else:
                    sp_.wait_ge(s_qk_in, 2 * HEADS)
                    sp_.wait_ge(s_v_in, HEADS)
            elif k0 == 0:
                sp_.wait_ge(s_q_ps, first_piece(5))
            w = peer_w_query[layer].rearrange("(k p) n -> p k n", p=P)
            for k in range(k0, k1):
                sp_.dma_start(wq[:, k, :], w[:, k, :]).then_inc(s_wq, 16)

        def raw_keys(layer, half):
            return hb[:, :].rearrange("p (a c) -> p a c", a=KD) if (layer, half) == (0, 1) else hbT

        def keys_sync(sp_, layer, half):
            if half == 0:
                if layer == 0:
                    sp_.wait_ge(s_att, 2 * HEADS)
                    sp_.wait_ge(s_conv, 8)
                else:
                    sp_.wait_ge(s_q_ps, first_piece(5))
                    sp_.wait_ge(s_hb, 5)
                sp_.dma_start(ffn_g[:, :], ffn_norm_g[layer:layer + 1, :].broadcast_to([P, D])).then_inc(s_ffng, 16)
            elif layer:
                sp_.wait_ge(s_keys_ps, 2 * layer + 1)
            for p_ in range(2):
                sp_.dma_start(raw_keys(layer, half)[:, 4 * p_:4 * p_ + 4, :],
                              peer_sub_keys[layer, p_, 4 * half:4 * half + 4, :, :].rearrange("h k c -> k h c")
                              ).then_inc(s_keys_raw[half], 16)

        def odd_weights_sync(sp_):
            sp_.wait_ge(s_proj, 2 * TILES)
            sp_.dma_start(odd_g[:, :], odd_norm_g[0:1, :].broadcast_to([P, D])).then_inc(s_oddw, 16)
            sp_.dma_start(pool_s[:, :], odd_pool_scale[0:1, :].broadcast_to([P, D])).then_inc(s_oddw, 16)
            for g in range(4):
                sp_.dma_start(pool_w[:, g, :, :], odd_pool_w[0, g].rearrange("(k p) n -> p k n", p=P)).then_inc(s_oddw, 16)
        ODD_LOADS = 6 * 16

        def save_parts(sp_, job, chunk, n_tokens):
            sp_.wait_ge(s_parts, job + 1)
            n = n_tokens // CHUNK
            for i in range(PARTS):
                sp_.dma_start(parts_dram[bass.ds(chunk, n), i, :, :], part[i][0:n_tokens, :]).then_inc(s_saved, 16)
            sp_.wait_ge(s_saved, 16 * PARTS * (job + 1))
            apart(sp_)

        def fetch_parts(sp_, u, par):
            wait(sp_, s_dot, CHUNK * (u - 1))
            sp_.dma_start(hparts[:, par, :], parts_dram[bass.ds(u, 1), :, :, :].rearrange("u a t d -> (u a t) d")).then_inc(s_fetched[par], 16)

        def mixer_constants(pool):
            c = Steps(pool, s_const)
            c.did(nc.gpsimd.memset(ident[:, :], 0.0))
            c.did(nc.gpsimd.memset(eps_col[:, :], EPS))
            c.did(nc.gpsimd.memset(causal[:, :], 1.0))
            c.did(nc.gpsimd.memset(neg[:, :], 0.0))
            c.did(nc.gpsimd.memset(neg_tri[:, :], -1.0))
            c.did(nc.gpsimd.memset(neg_ones[:, :], -1.0))
            c.did(nc.gpsimd.memset(neg_rest[:, :], -1.0))
            c.did(nc.gpsimd.memset(ident_b[:, :], 0.0))
            c.did(nc.gpsimd.memset(kT[0][:, :], 0.0))
            c.did(nc.gpsimd.memset(kT[1][:, :], 0.0))
            c.did(nc.gpsimd.memset(ss[:, :], 1.0))
            c.did(nc.gpsimd.memset(ssqk[:, :, :], 1.0))
            c.did(nc.gpsimd.memset(qkv[:, XT, :, :], 0.0))
            c.did(nc.gpsimd.memset(conv_in[:, :, 0:2], 0.0))
            c.settle()
            c.did(nc.gpsimd.affine_select(out=ident[:, :], in_=ident[:, :], compare_op=ALU.not_equal, fill=1.0,
                                          base=0, pattern=[[-1, P]], channel_multiplier=1))
            c.did(nc.gpsimd.affine_select(out=causal[:, :], in_=causal[:, :], compare_op=ALU.is_gt, fill=0.0,
                                          base=0, pattern=[[1, P]], channel_multiplier=-1))
            c.did(nc.gpsimd.affine_select(out=neg[:, :], in_=neg[:, :], compare_op=ALU.is_gt, fill=-BIG,
                                          base=0, pattern=[[1, P]], channel_multiplier=-1))
            c.did(nc.gpsimd.affine_select(out=neg_tri[:, :], in_=neg_tri[:, :], compare_op=ALU.is_ge, fill=0.0,
                                          base=0, pattern=[[-1, P]], channel_multiplier=1))
            c.did(nc.gpsimd.affine_select(out=neg_rest[:, :], in_=neg_rest[:, :], compare_op=ALU.is_gt, fill=0.0,
                                          base=0, pattern=[[1, P]], channel_multiplier=-1))
            c.did(nc.gpsimd.affine_select(out=ident_b[:, :], in_=ident_b[:, :], compare_op=ALU.not_equal, fill=1.0,
                                          base=0, pattern=[[-1, P]], channel_multiplier=1))
            return c.n
        MIXER_CONSTANTS = 20

        def expert_constants(pool):
            pool.wait_ge(s_att, 2 * HEADS)
            pool.wait_ge(s_conv, 8)
            nc.gpsimd.iota(iota16[:, :], pattern=[[1, TOPK]], base=0, channel_multiplier=0,
                           allow_small_or_imprecise_dtypes=True).then_inc(s_iota, 1)
            c = Steps(pool, s_setup)
            c.did(nc.gpsimd.memset(pick[:, :, :], 0.0))
            c.did(nc.gpsimd.memset(strip[:, :], 0.0))
            c.did(nc.gpsimd.memset(zeros[:, :], 0.0))
            c.did(nc.gpsimd.memset(prev[:, :], 0.0))
            for g, w in enumerate(WINDOWS):
                c.did(nc.gpsimd.memset(band[:, g, :], 1.0 / w))
                c.did(nc.gpsimd.memset(band_prev[:, g, :], 1.0 / w))
            c.settle()
            c.did(nc.gpsimd.affine_select(out=strip[:, :], in_=strip[:, :], compare_op=ALU.not_equal, fill=1.0,
                                          base=-(P - 1), pattern=[[1, 2 * P - 1]], channel_multiplier=0))
            for g, w in enumerate(WINDOWS):
                c.did(nc.gpsimd.affine_select(out=band[:, g, :], in_=band[:, g, :], compare_op=ALU.is_ge, fill=0.0,
                                              base=0, pattern=[[1, P]], channel_multiplier=-1))
                c.did(nc.gpsimd.affine_select(out=band_prev[:, g, :], in_=band_prev[:, g, :], compare_op=ALU.is_ge,
                                              fill=0.0, base=w - 1 - P, pattern=[[-1, P]], channel_multiplier=1))
            for i in range(PARTS):
                c.settle()
                c.did(nc.gpsimd.affine_select(out=pick[:, :, :], in_=pick[:, :, :], compare_op=ALU.not_equal, fill=1.0,
                                              base=-CHUNK * i, pattern=[[-1, CHUNK], [0, P]], channel_multiplier=1))
            c.settle()
            for g, w in enumerate(WINDOWS):
                c.did(nc.gpsimd.affine_select(out=band[:, g, :], in_=band[:, g, :], compare_op=ALU.is_ge, fill=0.0,
                                              base=w - 1, pattern=[[-1, P]], channel_multiplier=1))
            c.settle()
            for g in range(4):
                c.did(nc.gpsimd.tensor_tensor(band[:, g, :], band[:, g, :], ident[:, :], ALU.subtract))
            assert c.n == SETUP_STEPS, c.n
        SETUP_STEPS = 4 + 8 + 1 + 8 + PARTS + 4 + 4

        HALF = (SEQ + META) // 2
        CONV_COLS = [(META, META + HALF, 0, 0), (META + HALF, META + SEQ, 1, 0), (0, META, 1, SEQ - HALF)]

        def mixer_tensor(pe):
            pe.wait_ge(s_const, MIXER_CONSTANTS)

            def transpose_tile(t):
                n = rows_of(t)
                pe.wait_ge(s_xn, t + 1)
                if t >= 2:
                    pe.wait_ge(s_hT, 2 * (t - 1))
                for k in range(KD):
                    last = nc.tensor.transpose(psum[:, 2 * (t % 2) + k // 4, n * (k % 4):n * (k % 4) + n],
                                               xn[0:n, t % 2, P * k:P * k + P], ident[0:n, 0:n])
                last.then_inc(s_xnT, 1)

            transpose_tile(0)
            for g in range(3):
                pe.wait_ge(s_win[g % 2], 16 * (g // 2 + 1))
                for t in range(TILES):
                    if g == 0:
                        if t + 1 < TILES:
                            transpose_tile(t + 1)
                        pe.wait_ge(s_hT, 2 * (t + 1))
                    i = TILES * g + t
                    if i >= 4:
                        pe.wait_ge(s_qkv, i - 3)
                    n = rows_of(t)
                    for k in range(KD):
                        last = nc.tensor.matmul(psum[0:n, 4 + i % 4, :], hT[:, k, cols_of(t)], w_ring[:, g % 2, k, :],
                                                start=(k == 0), stop=(k == KD - 1))
                    last.then_inc(s_qkv_ps, 1)
            pe.wait_ge(s_qkv, 3 * TILES)
            def transpose_qk(h, par):
                pe.wait_ge(s_qk_in, 2 * h + 2)
                pe.wait_ge(s_v_in, h + 1)
                apart(pe)
                for i, src in enumerate((qs[par], ks[par])):
                    for t in range(TILES):
                        n = rows_of(t)
                        bank = 4 * par + 2 * i + t // XT
                        at = P * (t % XT)
                        last = nc.tensor.transpose(psum[0:DH, bank, at:at + n], src[0:n, t, :], ident[0:n, 0:n])
                last.then_inc(s_qkT_ps, 1)

            def scores(h, par):
                pe.wait_ge(s_qkT, 4 * h + 4)
                for b in KEY_BLOCKS + [XT]:
                    bank, at = Z_AT[b]
                    q0 = 0 if b == XT else P * b
                    nc.tensor.matmul(psum[:, 4 * par + bank, at:at + SEQ - q0], kT[par][:, P * b:P * b + P],
                                     qT[par][:, q0:SEQ], start=(at == 0), stop=True, skip_group_check=True)
                nc.tensor.matmul(psum[:, 4 * par + Z_META[0], Z_META[1]:Z_META[1] + META], kT[par][:, SEQ:SEQ + P],
                                 qT[par][:, SEQ:SEQ + META], start=False, stop=True,
                                 skip_group_check=True).then_inc(s_z, 1)

            def add(bank, cols, lhsT, rhs):
                return nc.tensor.matmul(psum[:, bank, cols], lhsT, rhs, start=False, stop=True, skip_group_check=True)

            def subtract_later(h, par, segment):
                pe.wait_ge(s_sp, 3 * h + segment + 1)
                for b in ((3, 2), (1,), (0,))[segment]:
                    bank, at = Z_AT[b]
                    bank += 4 * par
                    end = at + SEQ - P * b
                    add(bank, slice(at, end), neg_tri[:, :], z_cols(sp[par], b))
                    if b + 1 < XT:
                        add(bank, slice(at + P, end), neg_rest[:, :], z_cols(sp[par], b + 1))
                    last = add(bank, slice(at, at + P), ident_b[:, :], neg[:, :])
                if segment == 1:
                    bank, cols = 4 * par + Z_META[0], slice(Z_META[1], Z_META[1] + META)
                    add(bank, cols, neg_tri[0:META, :], sp[par][0:META, Z_META[0], cols])
                    last = add(bank, cols, ident_b[:, :], neg[:, 0:META])
                if segment == 2:
                    add(4 * par + 3, slice(0, SEQ), neg_tri[0:META, :], sp[par][0:META, 3, :])
                    last = add(4 * par + 3, slice(0, SEQ), neg_ones[:, :], z_cols(sp[par], 0))
                last.then_inc(s_S, 1)

            def attend(h, par):
                pe.wait_ge(s_v_in, h + 1)
                for segment, blocks in enumerate(((3, 2), (1,), (0, XT))):
                    pe.wait_ge(s_w, 3 * h + segment + 1)
                    for b in blocks:
                        q0, rows = (0, META) if b == XT else (P * b, P)
                        last = nc.tensor.matmul(psum[0:DH, 4 * par, q0:SEQ], vs[par][0:rows, b, :],
                                                z_cols(wts, b)[0:rows, :], start=(b == 3), stop=True, skip_group_check=True)
                nc.tensor.matmul(psum[0:DH, 4 * par + 1, 0:META], vs[par][0:META, XT, :],
                                 wts[0:META, Z_META[0], Z_META[1]:Z_META[1] + META], start=True, stop=True).then_inc(s_av, 1)

            def head(h, par, more=True):
                subtract_later(h, par, 0)
                if more:
                    transpose_qk(h + 1, 1 - par)
                subtract_later(h, par, 1)
                if more:
                    scores(h + 1, 1 - par)
                subtract_later(h, par, 2)
                attend(h, par)
            for g in range(3):
                if g == 2:
                    transpose_qk(0, 0)
                pe.wait_ge(s_win[(g + 3) % 2], 16 * ((g + 3) // 2 + 1))
                for m in range(4):
                    i = 4 * g + m
                    if i >= 2:
                        if i - 2 < 8:
                            pe.wait_ge(s_fm_a, 3 * (i - 1))
                        else:
                            pe.wait_ge(s_fm_u, 3 * (i - 2 - 7))
                    for k in range(KD):
                        w = w_ring[:, (g + 3) % 2, k, P * m:P * m + P]
                        for half in range(2):
                            last = nc.tensor.matmul(psum[:, 4 + 2 * (i % 2) + half, 0:HALF], w, hT[:, k, HALF * half:HALF * half + HALF],
                                                    start=(k == 0), stop=(k == KD - 1))
                    last.then_inc(s_fm_ps, 1)
                    if g == 2 and m == 0:
                        scores(0, 0)
            pe.wait_ge(s_fm_u, 12)
            with pe.Fori(0, HEADS // 2 - 1) as pair:
                head(2 * pair, 0)
                head(2 * pair + 1, 1)
            head(HEADS - 2, 0)
            head(HEADS - 1, 1, more=False)
            pe.wait_ge(s_att, 2 * HEADS)
            pe.wait_ge(s_conv, 8)
            pe.wait_ge(s_wout, 16)
            project_tensor(pe, 0)
            project_tensor(pe, 1)

        PROJECTED = [XT] + list(range(XT))

        def project_tensor(pe, i):
            t, half = PROJECTED[i // 2], i % 2
            if i >= 4:
                pe.wait_ge(s_mix, i - 3)
            for k in range(KD):
                last = nc.tensor.matmul(psum[0:rows_of(t), i % 4, :], catT[:, k, cols_of(t)],
                                        w_out_sb[:, k, 512 * half:512 * half + 512], start=(k == 0), stop=(k == KD - 1))
            last.then_inc(s_proj, 1)

        def add_projected(dve, i):
            dve.wait_ge(s_proj, i + 1)
            t, c = PROJECTED[i // 2], slice(512 * (i % 2), 512 * (i % 2) + 512)
            v = hres[0:rows_of(t), t, c]
            nc.vector.tensor_tensor(v, v, psum[0:rows_of(t), i % 4, :], ALU.add).then_inc(s_mix, 1)

        def mixer_scalar(act):
            nc.scalar.preload_act_table_set("natural_log_exp_and_others")
            act.wait_ge(s_const, MIXER_CONSTANTS)
            a = Steps(act, s_act)
            for t in range(TILES):
                n = rows_of(t)
                act.wait_ge(s_x[t], 16)
                a.did(nc.scalar.activation(sp[t % 2][0:n, 0:2, :].rearrange("p a b -> p (a b)"),
                                           hres[0:n, t, :], ACT.Square, accum_out=ss[0:n, t:t + 1]))
                a.settle()
            a.did(nc.scalar.activation(rstd[:, :], ss[:, :], ACT.Ln, scale=1.0 / D, bias=eps_col[:, :]))
            a.settle()
            nc.scalar.activation(rstd[:, :], rstd[:, :], ACT.Exp, scale=-0.5).then_inc(s_ss, 1)
            for g in range(3):
                for t in range(TILES):
                    i = TILES * g + t
                    n = rows_of(t)
                    act.wait_ge(s_qkv_ps, i + 1)
                    nc.scalar.copy(qkv[0:n, t, g, :], psum[0:n, 4 + i % 4, :]).then_inc(s_qkv, 1)
            act.wait_ge(s_ssqk, TILES)
            a.did(nc.scalar.activation(rqk[:, :, :], ssqk[:, :, :], ACT.Ln, scale=1.0 / DH, bias=eps_col[:, :]))
            a.settle()
            nc.scalar.activation(rqk[:, :, :], rqk[:, :, :], ACT.Exp, scale=-0.5).then_inc(s_rqk0, 1)
            for i in range(8):
                act.wait_ge(s_fm_ps, i + 1)
                dst = gate_b[:, i, :] if i < 4 else conv_in[:, i - 4, 2:2 + META + SEQ]
                for c0, c1, bank, b0 in CONV_COLS:
                    nc.scalar.copy(dst[:, c0:c1], psum[:, 4 + 2 * (i % 2) + bank, b0:b0 + c1 - c0]).then_inc(s_fm_a, 1)
            def take_v(h, par):
                if not (isinstance(h, int) and h < 2):
                    act.wait_ge(s_av, h - 1)
                nc.scalar.copy(vs[par][:, :, :], qkv[:, :, 2, bass.ts(h, DH)]).then_inc(s_v_in, 1)

            def copy_qk(h, par):
                act.wait_ge(s_qkT_ps, h + 1)
                for i, (dst, gain) in enumerate(((qT[par], qg8), (kT[par], kg))):
                    bank = 4 * par + 2 * i
                    nc.scalar.activation(dst[:, 0:SEQ], psum[0:DH, bank, :], ACT.Copy, scale=gain[:, 0:1]).then_inc(s_qkT, 1)
                    nc.scalar.activation(dst[:, SEQ:SEQ + META], psum[0:DH, bank + 1, 0:META], ACT.Copy,
                                         scale=gain[:, 0:1]).then_inc(s_qkT, 1)

            LOG_STEPS = ((ACT.Abs, 0, 0), (ACT.Abs, 1, 0), (ACT.Exp, 0, 1), (ACT.Abs, 2, 0), (ACT.Exp, 1, 2), (ACT.Ln, 0, 3),
                         (ACT.Exp, 2, 4), (ACT.Ln, 1, 5), (ACT.Ln, 2, 7))

            def log_terms(h, par, first, end):
                if first == 0:
                    act.wait_ge(s_z, h + 1)
                for func, segment, after in LOG_STEPS[first:end]:
                    banks, c0, c1 = SEGMENTS[segment]
                    dst = sp[par][:, banks, c0:c1]
                    src = dst
                    if func == ACT.Abs:
                        src = psum[:, banks.start + 4 * par:banks.stop + 4 * par, c0:c1]
                    else:
                        act.wait_ge(s_log, 9 * h + after)
                    nc.scalar.activation(dst, src, func, scale=-1.0 if func == ACT.Exp else 1.0,
                                         bias=1.0 if func == ACT.Ln else 0.0).then_inc(s_log, 1)

            def weights(h, par, segment):
                act.wait_ge(s_S, 3 * h + segment + 1)
                banks, c0, c1 = SEGMENTS[segment]
                nc.scalar.activation(wts[:, banks, c0:c1], psum[:, banks.start + 4 * par:banks.stop + 4 * par, c0:c1],
                                     ACT.Exp).then_inc(s_w, 1)

            def copy_out(h, par, block):
                act.wait_ge(s_av, h + 1)
                rows = slice(DH * par, DH * par + DH)
                nc.scalar.copy(catT[rows, block, 0:SEQ], psum[0:DH, 4 * par, :]).then_inc(s_att, 1)
                nc.scalar.copy(catT[rows, block, SEQ:SEQ + META], psum[0:DH, 4 * par + 1, 0:META]).then_inc(s_att, 1)

            def head(h, par, block, more=True, take=True):
                weights(h, par, 0)
                if more:
                    copy_qk(h + 1, 1 - par)
                weights(h, par, 1)
                if more:
                    log_terms(h + 1, 1 - par, 0, 6)
                weights(h, par, 2)
                if more:
                    log_terms(h + 1, 1 - par, 6, 8)
                copy_out(h, par, block)
                if take:
                    take_v(h + 2, par)
                if more:
                    log_terms(h + 1, 1 - par, 8, 9)
            take_v(0, 0)
            copy_qk(0, 0)
            log_terms(0, 0, 0, 9)
            take_v(1, 1)
            with act.Fori(0, HEADS // 2 - 1) as pair:
                head(2 * pair, 0, pair)
                head(2 * pair + 1, 1, pair)
            head(HEADS - 2, 0, HEADS // 2 - 1, take=False)
            head(HEADS - 1, 1, HEADS // 2 - 1, more=False, take=False)

        def mixer_vector(dve):
            dve.wait_ge(s_const, MIXER_CONSTANTS)
            d = Steps(dve, s_dve)
            dve.wait_ge(s_ss, 1)
            newton(dve, d, rstd[:, :], ss[:, :], D, rstd[:, :], s_rstd)
            dve.wait_ge(s_rstd, 1)
            dve.wait_ge(s_small, SMALL)
            for t in range(TILES):
                n = rows_of(t)
                dve.wait_ge(s_x[t], 16)
                if t >= 2:
                    dve.wait_ge(s_xnT, t - 1)
                nc.vector.tensor_scalar(xn[0:n, t % 2, :], hres[0:n, t, :], rstd[0:n, t:t + 1], None, ALU.mult).then_inc(s_xn, 1)
                dve.wait_ge(s_xnT, t + 1)
                for half in range(2):
                    nc.vector.tensor_tensor(hT[:, 4 * half:4 * half + 4, cols_of(t)],
                                            psum[:, 2 * (t % 2) + half, 0:4 * n].rearrange("p (k n) -> p k n", k=4),
                                            even_g[:, 4 * half:4 * half + 4].unsqueeze(2).to_broadcast([P, 4, n]),
                                            ALU.mult).then_inc(s_hT, 1)
            d.did(nc.vector.tensor_scalar(qg8[:, :], qg[:, :], DH ** -0.5, None, ALU.mult))
            dve.wait_ge(s_xnT, TILES)
            for t in range(TILES):
                n = rows_of(t)
                dve.wait_ge(s_qkv, TILES + t + 1)
                if t >= 2:
                    dve.wait_ge(s_ssqk, t - 1)
                qk = qkv[0:n, t, 0:2, :].rearrange("p a b -> p (a b)")
                d.did(nc.vector.tensor_tensor(xn[0:n, t % 2, :], qk, qk, ALU.mult))
                d.settle()
                nc.vector.tensor_reduce(ssqk[0:n, t, :], xn[0:n, t % 2, :].rearrange("p (h c) -> p h c", c=DH), AX.X,
                                        ALU.add).then_inc(s_ssqk, 1)
            dve.wait_ge(s_rqk0, 1)
            flat = rqk[:, :, :].rearrange("p a b -> p (a b)")
            newton(dve, d, flat, ssqk[:, :, :].rearrange("p a b -> p (a b)"), DH, flat, s_rqk)

            def convolve(m):
                dve.wait_ge(s_fm_a, 12 + 3 * m + 3)
                dve.wait_ge(s_fm_ps, 8 + m + 1)
                cin = conv_in[:, m, :]
                for c0, c1, bank, b0 in CONV_COLS:
                    src = psum[:, 4 + 2 * (m % 2) + bank, b0:b0 + c1 - c0]
                    nc.vector.tensor_tensor(cin[:, 2 + c0:2 + c1], cin[:, 2 + c0:2 + c1], src, ALU.mult).then_inc(s_fm_u, 1)
                dve.wait_ge(s_fm_u, 3 * m + 3)
                if m:
                    dve.wait_ge(s_conv, 2 * m)
                n = META + SEQ
                d.did(nc.vector.tensor_scalar(conv_y[:, :], cin[:, 0:n], conv_w[:, 0, m:m + 1], None, ALU.mult))
                d.settle()
                for i in (1, 2):
                    d.did(nc.vector.scalar_tensor_tensor(out=conv_y[:, :], in0=cin[:, i:i + n], scalar=conv_w[:, i, m:m + 1],
                                                         in1=conv_y[:, :], op0=ALU.mult, op1=ALU.add))
                    d.settle()
                nc.vector.tensor_tensor(catT[:, 4 + m, 0:SEQ], conv_y[:, META:n], gate_b[:, m, META:n], ALU.mult).then_inc(s_conv, 1)
                nc.vector.tensor_tensor(catT[:, 4 + m, SEQ:SEQ + META], conv_y[:, 0:META], gate_b[:, m, 0:META],
                                        ALU.mult).then_inc(s_conv, 1)
            dve.wait_ge(s_rqk, 1)
            HEAD_STEPS = 7

            def scale_qk(h, par):
                if not (isinstance(h, int) and h < 2):
                    dve.wait_ge(s_qkT_ps, h - 1)
                for i, dst in enumerate((qs[par], ks[par])):
                    scale = rqk[:, :, bass.ds(h + HEADS * i, 1)].to_broadcast([P, TILES, DH])
                    nc.vector.tensor_tensor(dst[:, :, :], qkv[:, :, i, bass.ts(h, DH)], scale, ALU.mult).then_inc(s_qk_in, 1)

            def softplus(h, par):
                s = Steps(dve, s_soft, HEAD_STEPS * h)
                for segment, logs in enumerate((6, 8, 9)):
                    banks, c0, c1 = SEGMENTS[segment]
                    dve.wait_ge(s_log, 9 * h + logs)
                    s.did(nc.vector.scalar_tensor_tensor(out=sp[par][:, banks, c0:c1],
                                                         in0=psum[:, banks.start + 4 * par:banks.stop + 4 * par, c0:c1], scalar=0.0,
                                                         in1=sp[par][:, banks, c0:c1], op0=ALU.max, op1=ALU.add))
                    s.settle()
                    if segment == 0:
                        v = z_cols(sp[par], 3)
                        s.did(nc.vector.tensor_tensor(v, v, causal[:, :], ALU.mult))
                    if segment == 1:
                        v = sp[par][0:META, Z_META[0], Z_META[1]:Z_META[1] + META]
                        nc.vector.tensor_tensor(v, v, causal[0:META, 0:META], ALU.mult)
                    b = 2 - segment
                    v = z_cols(sp[par], b)[:, 0:P]
                    s.did(nc.vector.tensor_tensor(v, v, causal[:, :], ALU.mult))
                    if segment:
                        dve.wait_ge(s_sp, 3 * h + segment)
                    else:
                        s.settle()
                    v = z_cols(sp[par], b)[:, P:]
                    nc.vector.tensor_tensor(v, v, z_cols(sp[par], b + 1), ALU.add).then_inc(s_sp, 1)
                assert s.n == HEAD_STEPS

            scale_qk(0, 0)
            scale_qk(1, 1)
            convolve(0)
            softplus(0, 0)
            for m in range(1, 4):
                convolve(m)
            scale_qk(2, 0)
            with dve.Fori(0, HEADS // 2 - 2) as pair:
                softplus(2 * pair + 1, 1)
                scale_qk(2 * pair + 3, 1)
                softplus(2 * pair + 2, 0)
                scale_qk(2 * pair + 4, 0)
            softplus(HEADS - 3, 1)
            scale_qk(HEADS - 1, 1)
            softplus(HEADS - 2, 0)
            softplus(HEADS - 1, 1)
            add_projected(dve, 0)
            add_projected(dve, 1)

        def keys_tensor(pe, layer, half):
            pe.wait_ge(s_keys_raw[half], 32 * (layer + 1))
            wait(pe, s_keys, 2 * (2 * layer + half))
            if layer and not half:
                pe.wait_ge(s_routed, first_piece(5) + 1)
                pe.wait_ge(s_idx, 5)
            for i in range(8):
                last = nc.tensor.transpose((FA, FB)[i // 4][:, P * (i % 4):P * (i % 4) + P],
                                           raw_keys(layer, half)[:, i, :], ident[:, :])
            last.then_inc(s_keys_ps, 1)

        def keys_scalar(act, layer, half):
            lists = keysT[:, :, :].rearrange("c (h a) k -> c a h k", a=2)
            act.wait_ge(s_keys_ps, 2 * layer + half + 1)
            for p_ in range(2):
                nc.scalar.copy(lists[:, p_, 4 * half:4 * half + 4, :],
                               (FA, FB)[p_].rearrange("p (h k) -> p h k", h=4)).then_inc(s_keys, 1)

        def norm_scalar(act, job, n, src):
            wait(act, s_parts, job)
            wait(act, s_saved, 16 * PARTS * job)
            apart(act)
            nc.scalar.activation(part[0][0:n, :], src, ACT.Square, accum_out=ss[0:n, 0:1]).then_inc(s_hsq, 1)
            act.wait_ge(s_hsq, 2 * job + 1)
            nc.scalar.activation(rstd[0:n, 0:1], ss[0:n, 0:1], ACT.Ln, scale=1.0 / D, bias=eps_col[0:n, :]).then_inc(s_hsq, 1)
            act.wait_ge(s_hsq, 2 * job + 2)
            nc.scalar.activation(rstd[0:n, 0:1], rstd[0:n, 0:1], ACT.Exp, scale=-0.5).then_inc(s_hguess, 1)

        def transposed_scalar(act, job, n):
            act.wait_ge(s_hbT_ps, job + 1)
            for half in range(2):
                nc.scalar.copy(hbT[:, 4 * half:4 * half + 4, 0:n],
                               (FA, FB)[half][:, 0:4 * n].rearrange("p (k n) -> p k n", k=4)).then_inc(s_hbT, 1)

        def norm_vector(dve, job, n, src, layer):
            dve.wait_ge(s_hguess, job + 1)
            newton(dve, Steps(dve, s_hnewton, (NEWTON + 1) * job), rstd[0:n, 0:1], ss[0:n, 0:1], D, rstd[0:n, 0:1], s_hnewton)
            dve.wait_ge(s_hnewton, (NEWTON + 1) * (job + 1))
            dve.wait_ge(s_ffng, 16 * (layer + 1))
            dve.wait_ge(s_keys_ps, 2)
            nc.vector.scalar_tensor_tensor(out=hb[0:n, :], in0=src, scalar=rstd[0:n, 0:1], in1=ffn_g[0:n, :],
                                           op0=ALU.mult, op1=ALU.mult).then_inc(s_hb, 1)
            dve.wait_ge(s_hb, job + 1)

        def split_vector(dve, job, n, step):
            if step == 1:
                dve.wait_ge(s_hbT_ps, job + 1)
            if step:
                dve.wait_ge(s_split, SPLIT * job + step)
            if step % 2 == 0:
                nc.vector.tensor_copy(part[step // 2][0:n, :], hb[0:n, :]).then_inc(s_split if step < SPLIT else s_parts, 1)
            else:
                nc.vector.tensor_tensor(hb[0:n, :], hb[0:n, :], part[step // 2][0:n, :], ALU.subtract).then_inc(s_split, 1)

        def start_tensor(pe, job, n, layer):
            pe.wait_ge(s_hb, job + 1)
            pe.wait_ge(s_keys, 4 * (layer + 1))
            pe.wait_ge(s_wq, 16 * KD * (layer + 1))
            if isinstance(job, int) and job == 1:
                pe.wait_ge(s_spread, GROUPS)
            elif not isinstance(job, int) or job > 1:
                pe.wait_ge(s_routed, first_piece(job) + 1)
                pe.wait_ge(s_idx, job)
            wait(pe, s_hbT, 2 * job)
            wait(pe, s_qT, first_piece(job))
            for k in range(KD):
                last = nc.tensor.transpose((FA, FB)[k // 4][:, n * (k % 4):n * (k % 4) + n], hb[0:n, P * k:P * k + P],
                                           ident[0:n, 0:n])
            last.then_inc(s_hbT_ps, 1)

        def query_tensor(pe, piece, s, n, k0, k1, dst):
            for k in range(k0, k1):
                ins = nc.tensor.matmul(dst[0:n, :], hbT[:, k, 0:n], wq[:, k, bass.ts(s, 512)],
                                       start=(k == 0), stop=(k == KD - 1))
            if k1 == KD:
                ins.then_inc(s_q_ps, 1)

        def query_scalar(act, piece, n, src):
            act.wait_ge(s_q_ps, piece + 1)
            nc.scalar.copy(q_sb[0:n, :], src[0:n, :]).then_inc(s_q, 1)

        def queryT_tensor(pe, piece, n):
            pe.wait_ge(s_q, piece)
            apart(pe)
            for i in range(LISTS):
                last = nc.tensor.transpose(FB[:, n * i:n * i + n], q_sb[0:n, P * i:P * i + P], ident[0:n, 0:n])
            last.then_inc(s_qT_ps, 1)

        def queryT_scalar(act, piece, n):
            act.wait_ge(s_qT_ps, piece)
            nc.scalar.copy(q_T[:, :, 0:n], FB[:, 0:LISTS * n].rearrange("p (a n) -> p a n", a=LISTS)).then_inc(s_qT, 1)

        GROUPS = HEADS // 2
        META_BANKS = [psum[:, 4 + g, :] for g in range(GROUPS)]
        META_Q = [gateT[0:META, 0:512], gateT[0:META, 512:1024], q_sb[0:META, :], work[0:META, :]]
        metaT = q_T[:, :, :].rearrange("p a n -> p (a n)")[:, 0:LISTS * GROUPS * META]

        def meta_queries_tensor(pe):
            pe.wait_ge(s_hbT, 2)
            for g in range(GROUPS):
                for k in range(KD):
                    last = nc.tensor.matmul(META_BANKS[g][0:META, :], hbT[:, k, 0:META], wq[:, k, 512 * g:512 * g + 512],
                                            start=(k == 0), stop=(k == KD - 1))
                last.then_inc(s_meta_q_ps, 1)
            for g in range(GROUPS):
                pe.wait_ge(s_meta_q, g + 1)
                for i in range(LISTS):
                    at = META * (LISTS * g + i)
                    last = nc.tensor.transpose(QUERY_BANK[:, at:at + META], META_Q[g][:, P * i:P * i + P], ident[0:META, 0:META])
            last.then_inc(s_q_ps, 1)

        def meta_scores_tensor(pe):
            pe.wait_ge(s_qT, 1)
            for i in range(LISTS * GROUPS):
                at = P * (i % LISTS)
                last = nc.tensor.matmul(META_BANKS[i // LISTS][0:META, at:at + P], metaT[:, META * i:META * i + META],
                                        keysT[:, i, :], start=True, stop=True)
            last.then_inc(s_sc, 1)

        def meta_scalar(act):
            for g in range(GROUPS):
                act.wait_ge(s_meta_q_ps, g + 1)
                nc.scalar.copy(META_Q[g], META_BANKS[g][0:META, :]).then_inc(s_meta_q, 1)
            act.wait_ge(s_q_ps, 1)
            nc.scalar.copy(metaT, QUERY_BANK[:, 0:LISTS * GROUPS * META]).then_inc(s_qT, 1)
            act.wait_ge(s_cleared, 1)
            act.wait_ge(s_sc, 1)
            for g in range(GROUPS):
                nc.scalar.copy(cand[32 * g:32 * g + META, :], META_BANKS[g][0:META, :]).then_inc(s_spread, 1)

        def meta_tail_tensor(pe):
            pe.wait_ge(s_gate, 1)
            w = 2 * TOPK
            nc.tensor.transpose(META_BANKS[1][0:w, 0:P], soft[:, 0:w], ident[:, :])
            nc.tensor.transpose(META_BANKS[1][0:w, P:2 * P], top_i[:, 0:w], ident[:, :]).then_inc(s_gateT, 1)

        def meta_tables_scalar(act):
            act.wait_ge(s_gateT, 1)
            both = META_BANKS[1][0:2 * TOPK, 0:2 * P].rearrange("p (a n) -> p a n", a=2)
            for g in range(GROUPS):
                nc.scalar.copy(meta_tables[32 * g:32 * g + 32, :].rearrange("p (a n) -> p a n", a=2),
                               both[:, :, 32 * g:32 * g + META]).then_inc(s_spread, 1)

        def meta_tables_vector(dve):
            dve.wait_ge(s_spread, 2 * GROUPS)
            nc.vector.tensor_copy(gateT[:, 0:META], meta_tables[:, 0:META])
            nc.vector.tensor_scalar(idxT[:, 0:META], meta_tables[:, META:2 * META], 0.0, None, ALU.add).then_inc(s_idx, 1)

        def scores_tensor(pe, piece, s, n):
            pe.wait_ge(s_qT, piece + 1)
            for i in range(LISTS):
                lists = keysT[:, bass.ds(LISTS * s + i, 1), :].rearrange("p a k -> p (a k)")
                last = nc.tensor.matmul(FA[0:n, P * i:P * i + P], q_T[:, i, 0:n], lists, start=True, stop=True)
            last.then_inc(s_sc, 1)
        s_read = sem("key_scores_read")
        s_meta_q_ps = sem("meta_queries_multiplied")
        s_meta_q = sem("meta_queries_copied")
        s_cleared = sem("meta_rows_cleared")
        s_spread = sem("meta_rows_spread")
        s_routed_in = sem("key_numbers_as_floats")
        s_onehot = sem("onehot_step")

        def topk_stages(dve, piece, s, n, meta=False):
            c = Steps(dve, s_topk, TOPK_STEPS * piece)
            e = Steps(dve, s_onehot, 8 * piece)
            r = slice(0, n)
            lists = [(cand if meta else FA)[r, P * i:P * i + P] for i in range(LISTS)]
            works = [work[r, P * i:P * i + P] for i in range(LISTS)]
            cands = [cand[r, 256 * h:256 * h + 256] for h in range(2)]
            cworks = [work[r, 256 * h:256 * h + 256] for h in range(2)]
            cand4 = cand[r, :].rearrange("p (h a b) -> p h a b", h=2, a=TOPK)
            work4 = work[r, :].rearrange("p (h a b) -> p h a b", h=2, a=TOPK)

            def best8(vals, src):
                c.settle()
                apart(dve)
                for i in range(len(src)):
                    c.did(nc.vector.max(vals[r, i, 0:8], src[i]))

            def numbers8(vals, idx, src, dst, done=None):
                c.settle()
                apart(dve)
                for i in range(len(src)):
                    c.did(nc.vector.max_index(idx[r, i, 0:8], vals[r, i, 0:8], src[i]))
                for i in range(len(src)):
                    ins = nc.vector.match_replace(dst[i], vals[r, i, 0:8], src[i], -3e38)
                    if done is not None and i == len(src) - 1:
                        ins.then_inc(done, 1)
                    else:
                        c.did(ins)

            def next8(vals, dst):
                c.settle()
                apart(dve)
                for i in range(len(dst)):
                    c.did(nc.vector.max(vals[r, i, 8:16], dst[i]))

            def next_numbers8(vals, idx, dst):
                c.settle()
                apart(dve)
                for i in range(len(dst)):
                    c.did(nc.vector.max_index(idx[r, i, 8:16], vals[r, i, 8:16], dst[i]))

            def lists_best():
                if meta:
                    dve.wait_ge(s_spread, GROUPS)
                else:
                    dve.wait_ge(s_sc, piece + 1)
                apart(dve)
                for i in range(LISTS):
                    c.did(nc.vector.max(sv[r, i, 0:8], lists[i]))

            def lists_numbers():
                numbers8(sv, si, lists, works, s_read)
                dve.wait_ge(s_read, piece + 1)

            def sums():
                c.settle()
                v = sv[r, :, :].rearrange("p (h a) k -> p h a k", a=2)
                for h in range(2):
                    c.did(nc.vector.tensor_tensor(cand4[:, h], v[:, h, 0, :].unsqueeze(2).to_broadcast([n, TOPK, TOPK]),
                                                  v[:, h, 1, :].unsqueeze(1).to_broadcast([n, TOPK, TOPK]), ALU.add))
                nc.vector.tensor_copy(sif[r, :, :], si[r, :, :]).then_inc(s_routed_in, 1)

            def split_places():
                c.settle()
                nc.vector.tensor_copy(top_s[r, bass.ts(s, 2 * TOPK)], tv[r, :, :].rearrange("p a b -> p (a b)"))
                c.did(nc.vector.tensor_scalar(ta[r, :, :], tpos[r, :, :], 4, None, ALU.logical_shift_right))
                c.did(nc.vector.tensor_scalar(tb[r, :, :], tpos[r, :, :], TOPK - 1, None, ALU.bitwise_and))
                c.settle()
                for src, hot in ((ta, cand4), (tb, work4)):
                    for h in range(2):
                        e.did(nc.vector.tensor_tensor(hot[:, h], src[r, h, :].unsqueeze(2).to_broadcast([n, TOPK, TOPK]),
                                                      iota16[r, :].unsqueeze(1).to_broadcast([n, TOPK, TOPK]), ALU.is_equal))

            def look_up():
                e.settle()
                dve.wait_ge(s_routed_in, piece + 1)
                for a_, hot in ((0, cand4), (1, work4)):
                    for h in range(2):
                        e.did(nc.vector.tensor_tensor(hot[:, h], hot[:, h],
                                                      sif[r, 2 * h + a_, :].unsqueeze(1).to_broadcast([n, TOPK, TOPK]), ALU.mult))

            def add_up():
                e.settle()
                nc.vector.tensor_reduce(ia[r, :, :], cand4, AX.X, ALU.add)
                c.did(nc.vector.tensor_reduce(ib[r, :, :], work4, AX.X, ALU.add))

            def number():
                c.settle()
                nc.vector.scalar_tensor_tensor(out=top_i[r, bass.ts(s, 2 * TOPK)], in0=ia[r, :, :].rearrange("p a b -> p (a b)"),
                                               scalar=float(NKEYS), in1=ib[r, :, :].rearrange("p a b -> p (a b)"),
                                               op0=ALU.mult, op1=ALU.add).then_inc(s_routed, 1)
                dve.wait_ge(s_routed, piece + 2)
                assert c.n == TOPK_STEPS and e.n == 8, c.n

            return [lists_best, lists_numbers, lambda: next8(sv, works), lambda: next_numbers8(sv, si, works), sums,
                    lambda: best8(tv, cands), lambda: numbers8(tv, tpos, cands, cworks), lambda: next8(tv, cworks),
                    lambda: next_numbers8(tv, tpos, cworks), split_places, look_up, add_up, number]
        TOPK_STAGES = 13

        def logits_vector(dve, job, n, heads=HEADS):
            r = slice(0, n)
            dve.wait_ge(s_routed, first_piece(job + 1) + 1)
            t3 = top_s[r, 0:TOPK * heads].rearrange("p (h k) -> p h k", k=TOPK)
            s3 = soft[r, 0:TOPK * heads].rearrange("p (h k) -> p h k", k=TOPK)
            nc.vector.tensor_tensor(s3, t3, t3[:, :, 0:1].to_broadcast([n, heads, TOPK]), ALU.subtract).then_inc(s_exp_in, 1)

        def gates_vector(dve, job, n, heads=HEADS):
            r = slice(0, n)
            s3 = soft[r, 0:TOPK * heads].rearrange("p (h k) -> p h k", k=TOPK)
            dve.wait_ge(s_exp, job + 1)
            c = Steps(dve, s_tail, GATE_STEPS * job)
            c.did(nc.vector.tensor_reduce(soft_sum[r, 0:heads], s3, AX.X, ALU.add))
            c.settle()
            c.did(nc.vector.reciprocal(soft_r[r, 0:heads], soft_sum[r, 0:heads]))
            c.settle()
            nc.vector.tensor_tensor(s3, s3, soft_r[r, 0:heads].unsqueeze(2).to_broadcast([n, heads, TOPK]), ALU.mult).then_inc(s_gate, 1)

        def tables_vector(dve, job, n, col, layer):
            dve.wait_ge(s_gateT, job + 1)
            nc.vector.tensor_copy(gateT[:, bass.ds(col, n)], FB[:, 0:n])
            nc.vector.tensor_scalar(idxT[:, bass.ds(col, n)], FB[:, P:P + n], float(EXPERTS * layer), None,
                                    ALU.add).then_inc(s_idx, 1)

        def tail_scalar(act, job, n, heads=HEADS):
            act.wait_ge(s_exp_in, job + 1)
            nc.scalar.activation(soft[0:n, 0:TOPK * heads], soft[0:n, 0:TOPK * heads], ACT.Exp).then_inc(s_exp, 1)

        def tail_tensor(pe, job, n):
            pe.wait_ge(s_gate, job + 1)
            apart(pe)
            nc.tensor.transpose(FB[:, 0:n], soft[0:n, :], ident[0:n, 0:n])
            nc.tensor.transpose(FB[:, P:P + n], top_i[0:n, :], ident[0:n, 0:n]).then_inc(s_gateT, 1)

        def pool_norm_scalar(act, k, jobs, n, src):
            act.wait_ge(s_yadd, k + 1)
            act.wait_ge(s_parts, jobs)
            act.wait_ge(s_saved, 16 * PARTS * jobs)
            apart(act)
            nc.scalar.activation(part[0][0:n, :], src, ACT.Square, accum_out=ss[0:n, 0:1]).then_inc(s_psq, 1)
            act.wait_ge(s_psq, 2 * k + 1)
            nc.scalar.activation(rstd[0:n, 0:1], ss[0:n, 0:1], ACT.Ln, scale=1.0 / D, bias=eps_col[0:n, :]).then_inc(s_psq, 1)
            act.wait_ge(s_psq, 2 * k + 2)
            nc.scalar.activation(rstd[0:n, 0:1], rstd[0:n, 0:1], ACT.Exp, scale=-0.5).then_inc(s_pguess, 1)

        def pool_norm_vector(dve, k, n, src):
            dve.wait_ge(s_oddw, ODD_LOADS)
            if not (isinstance(k, int) and k == 0):
                dve.wait_ge(s_prev_meta, 16)
            dve.wait_ge(s_pguess, k + 1)
            newton(dve, Steps(dve, s_pool, POOL_STEPS * k), rstd[0:n, 0:1], ss[0:n, 0:1], D, rstd[0:n, 0:1], s_pool)
            dve.wait_ge(s_pool, POOL_STEPS * (k + 1))
            nc.vector.scalar_tensor_tensor(out=hb[0:n, :], in0=src, scalar=rstd[0:n, 0:1], in1=odd_g[0:n, :],
                                           op0=ALU.mult, op1=ALU.mult).then_inc(s_hf, 1)

        def meta_prev_sync(sp_):
            sp_.wait_ge(s_hf, 1)
            sp_.wait_ge(s_setup, SETUP_STEPS)
            sp_.dma_start(prev[P - META:P, :], hb[0:META, :]).then_inc(s_prev_meta, 16)
        s_prev_meta = sem("meta_rows_placed")

        def pool_diff_tensor(pe, k, job, g):
            if g == 0:
                pe.wait_ge(s_hf, k + 1)
                pe.wait_ge(s_prev_meta, 16)
                pe.wait_ge(s_oddw, ODD_LOADS)
                pe.wait_ge(s_setup, SETUP_STEPS)
                pe.wait_ge(s_routed, first_piece(job) + 1)
                pe.wait_ge(s_idx, job)
                pe.wait_ge(s_keys, 8)
            for c in (2 * g, 2 * g + 1):
                dst = (FA, FB)[c // 4][:, P * (c % 4):P * (c % 4) + P]
                nc.tensor.matmul(dst, hb[:, P * c:P * c + P], band[:, c // 2, :], start=True, stop=False)
                last = nc.tensor.matmul(dst, prev[:, P * c:P * c + P], band_prev[:, c // 2, :], start=False, stop=True)
            if g == 3:
                last.then_inc(s_dT_ps, 1)

        def pool_mix_tensor(pe, k, g):
            if g == 0:
                pe.wait_ge(s_dT, 2 * k)
            for c in range(2):
                last = nc.tensor.matmul((FA, FB)[g // 2][:, 256 * (g % 2):256 * (g % 2) + 256], hbT[:, 2 * g + c, :],
                                        pool_w[:, g, c, :], start=(c == 0), stop=(c == 1))
            if g == 3:
                last.then_inc(s_py, 1)

        def pool_scalar(act, k):
            act.wait_ge(s_dT_ps, k)
            for half in range(2):
                nc.scalar.copy(hbT[:, 4 * half:4 * half + 4, :],
                               (FA, FB)[half].rearrange("p (k n) -> p k n", k=4)).then_inc(s_dT, 1)
            nc.scalar.copy(prev[:, :], hb[:, :]).then_inc(s_prev, 1)

        def pool_vector(dve, k, dst):
            dve.wait_ge(s_py, k)
            dve.wait_ge(s_prev, k)
            for half in range(2):
                c = slice(512 * half, 512 * half + 512)
                nc.vector.tensor_tensor(hb[:, c], (FA, FB)[half], pool_s[:, c], ALU.mult).then_inc(s_pmul, 1)
            dve.wait_ge(s_pmul, 2 * k)
            nc.vector.tensor_tensor(dst, dst, hb[:, :], ALU.add).then_inc(s_padd, 1)
            dve.wait_ge(s_padd, k)
        s_pmul = sem("pool_scaled")

        u_rows = peer_u.rearrange("l e d -> (l e) d")
        v_rows = peer_v.rearrange("l e d -> (l e) d")

        def gather_pool(pool, u, v, par):
            if u is not None:
                pool.wait_ge(s_idx_u, u + 1)
            if v is not None:
                pool.wait_ge(s_idx_v, v + 1)
            for i in range(CHUNK):
                if u is not None:
                    wait(pool, s_dot, CHUNK * u + i + 1 - U_SLOTS)
                if v is not None:
                    wait(pool, s_acc, CHUNK * v + i + 1 - V_SLOTS)
                apart(pool)
                if u is not None:
                    nc.gpsimd.indirect_dma_start(u_ring[:, i % U_SLOTS, :], None, u_rows,
                                                 bass.IndirectOffsetOnAxis(idx_u[par][:, i:i + 1], 0)
                                                 ).then_inc(s_u[i % U_SLOTS], 16)
                if v is not None:
                    nc.gpsimd.indirect_dma_start(v_ring[:, i % V_SLOTS, :], None, v_rows,
                                                 bass.IndirectOffsetOnAxis(idx_v[par][:, i:i + 1], 0)
                                                 ).then_inc(s_v[i % V_SLOTS], 16)

        def at_token(hooks, i):
            for at, step in hooks:
                if at == i:
                    step()

        def experts_tensor(pe, u, v, par, fetched, hooks=()):
            if u is not None:
                pe.wait_ge(s_fetched[par], 16 * fetched)
            for i in range(CHUNK):
                if u is not None:
                    wait(pe, s_dot, CHUNK * u + i - 1)
                    for half in range(2):
                        ins = nc.tensor.matmul(bc[i % 2][:, half, :], pick[:, i, :],
                                               hparts[:, par, 512 * half:512 * half + 512], start=True, stop=True)
                    ins.then_inc(s_bc, 1)
                if v is not None:
                    pe.wait_ge(s_v[i % V_SLOTS], 16 * ((CHUNK // V_SLOTS) * v + i // V_SLOTS + 1))
                    pe.wait_ge(s_wcol, CHUNK * v + i + 1)
                    for half in range(2):
                        ins = nc.tensor.matmul(y_ps[:, half, :], w_col[:, i % W_SLOTS, :],
                                               v_ring[:, i % V_SLOTS, 512 * half:512 * half + 512],
                                               start=False, stop=False, skip_group_check=True)
                    ins.then_inc(s_acc, 1)
                at_token(hooks, i)

        def open_sum(pe, tiles):
            wait(pe, s_yadd, tiles)
            pe.wait_ge(s_setup, SETUP_STEPS)
            for half in range(2):
                nc.tensor.matmul(y_ps[:, half, :], zeros[:, 0:P], zeros[:, :], start=True, stop=False, skip_group_check=True)

        def close_sum(pe):
            for half in range(2):
                ins = nc.tensor.matmul(y_ps[:, half, :], zeros[:, 0:P], zeros[:, :], start=False, stop=True, skip_group_check=True)
            ins.then_inc(s_y, 1)

        def stage_u(act, u, par):
            wait(act, s_dot, CHUNK * (u - 1))
            apart(act)
            nc.scalar.copy(idx_u[par][:, :], idxT[:, bass.ds(CHUNK * u, CHUNK)]).then_inc(s_idx_u, 1)

        def stage_v(act, v, par):
            wait(act, s_acc, CHUNK * (v - 1))
            apart(act)
            nc.scalar.copy(idx_v[par][:, :], idxT[:, bass.ds(CHUNK * v, CHUNK)]).then_inc(s_idx_v, 1)

        def gelu_scalar(act, u):
            act.wait_ge(s_garg, u + 1)
            wait(act, s_weight, u)
            nc.scalar.activation(ge[:, :], ga[:, :], ACT.Exp, scale=-1.0).then_inc(s_gexp, 1)

        def columns_scalar(act, v, par, pos, hooks=()):
            act.wait_ge(s_weight, v + 1)
            for i in range(CHUNK):
                wait(act, s_acc, CHUNK * v + i + 1 - W_SLOTS)
                nc.scalar.activation(w_col[:, i % W_SLOTS, :], strip[:, bass.ds(P - 1 - i - pos, P)], ACT.Copy,
                                     scale=weight[par][:, i:i + 1]).then_inc(s_wcol, 1)
                at_token(hooks, i)

        def gelu_argument(dve, u, par):
            c = Steps(dve, s_gelu, (GELU1 + GELU2) * u)
            dve.wait_ge(s_dot, CHUNK * (u + 1))
            if not (isinstance(u, int) and u == 0):
                dve.wait_ge(s_gexp, u)
            c.did(nc.vector.tensor_tensor(ga[:, :], dot[par][:, :], dot[par][:, :], ALU.mult))
            c.settle()
            c.did(nc.vector.tensor_scalar(ga[:, :], ga[:, :], GELU_B, GELU_A, ALU.mult, ALU.add))
            c.settle()
            c.did(nc.vector.tensor_tensor(ga[:, :], ga[:, :], dot[par][:, :], ALU.mult))
            c.settle()
            nc.vector.tensor_scalar(ga[:, :], ga[:, :], -80.0, None, ALU.max).then_inc(s_garg, 1)

        def gelu_weights(dve, u, par):
            c = Steps(dve, s_gelu, (GELU1 + GELU2) * u + GELU1)
            wait(dve, s_weight, u)
            c.did(nc.vector.tensor_tensor(gx[:, :], dot[par][:, :], gateT[:, bass.ds(CHUNK * u, CHUNK)], ALU.mult))
            dve.wait_ge(s_gexp, u + 1)
            c.did(nc.vector.tensor_scalar(ge[:, :], ge[:, :], 1.0, None, ALU.add))
            c.settle()
            c.did(nc.vector.reciprocal(ge[:, :], ge[:, :]))
            c.settle()
            wait(dve, s_wcol, CHUNK * (u - 1))
            nc.vector.tensor_tensor(weight[par][:, :], gx[:, :], ge[:, :], ALU.mult).then_inc(s_weight, 1)

        def dots_vector(dve, u, par, hooks=(), first=False):
            for i in range(CHUNK):
                dve.wait_ge(s_u[i % U_SLOTS], 16 * ((CHUNK // U_SLOTS) * u + i // U_SLOTS + 1))
                dve.wait_ge(s_bc, CHUNK * u + i + 1)
                row = u_ring[:, i % U_SLOTS, :]
                nc.vector.scalar_tensor_tensor(out=row, in0=row, scalar=1.0, in1=bc[i % 2].rearrange("p a b -> p (a b)"),
                                               op0=ALU.mult, op1=ALU.mult, accum_out=dot[par][:, i:i + 1]).then_inc(s_dot, 1)
                if i == 3 and not first:
                    gelu_weights(dve, u - 1, 1 - par)
                at_token(hooks, i)
            gelu_argument(dve, u, par)

        def take_sum(dve, tiles, dst, n):
            dve.wait_ge(s_y, tiles + 1)
            nc.vector.tensor_tensor(dst, dst, y_ps[0:n, :, :].rearrange("p a b -> p (a b)"), ALU.add).then_inc(s_yadd, 1)
            dve.wait_ge(s_yadd, tiles + 1)

        def tile_of(slot, n=P):
            return hres[0:n, bass.ds(slot, 1), :].rearrange("p a d -> p (a d)")

        LAST = 2 * XT - 1
        QUERY_BANK = psum[:, 4, :]

        def halves(hooks):
            return [(at, f) for at, f in hooks if at < CHUNK], [(at - CHUNK, f) for at, f in hooks if at >= CHUNK]

        QUERIED = (6, 18)
        SCORED = (8, 20)

        def routing_tensor(pe, job, s):
            p0 = first_piece(job) + 2 * s

            def query(e, k):
                def step():
                    if k == 0:
                        pe.wait_ge(s_read, p0 + e)
                        pe.wait_ge(s_hbT, 2 * job + 2)
                    query_tensor(pe, p0 + e, 2 * s + e, P, k, k + 1, FA)
                return step

            hooks = []
            for e in range(2):
                hooks += [(max(QUERIED[e] + 1 - KD + k, 0), query(e, k)) for k in range(KD)]
                hooks += [(QUERIED[e] + 1, lambda e=e: queryT_tensor(pe, p0 + e, P)),
                          (SCORED[e], lambda e=e: scores_tensor(pe, p0 + e, 2 * s + e, P))]
            return halves(hooks)

        def routing_scalar(act, job, s):
            p0 = first_piece(job) + 2 * s
            hooks = []
            for e in range(2):
                hooks += [(QUERIED[e], lambda e=e: query_scalar(act, p0 + e, P, FA)),
                          (QUERIED[e] + 1, lambda e=e: queryT_scalar(act, p0 + e, P))]
            return halves(hooks)

        def routing_vector(dve, job, s):
            p0 = first_piece(job) + 2 * s
            hooks = []
            for e, end in ((0, SCORED[1]), (1, 2 * CHUNK - 1)):
                stages = topk_stages(dve, p0 + e, 2 * s + e, P)
                hooks += [(min(SCORED[e] + 1 + i, end), stages[i]) for i in range(TOPK_STAGES)]
            return halves(hooks)

        def start_stages_tensor(pe, job, k):
            if k is None:
                return halves([(3, lambda: start_tensor(pe, job, P, 0))])
            return halves([(2 + g, lambda g=g: pool_diff_tensor(pe, k, job, g)) for g in range(4)] +
                          [(6 + g, lambda g=g: pool_mix_tensor(pe, k, g)) for g in range(4)] +
                          [(13, lambda: start_tensor(pe, job, P, 1))])

        def start_stages_scalar(act, job, k, src):
            def norm():
                if k is not None:
                    act.wait_ge(s_padd, k)
                norm_scalar(act, job, P, src)
            if k is None:
                return halves([(0, norm), (4, lambda: transposed_scalar(act, job, P))])
            return halves([(0, lambda: pool_norm_scalar(act, k, job, P, src)), (5, lambda: pool_scalar(act, k)), (11, norm),
                           (14, lambda: transposed_scalar(act, job, P))])

        def start_stages_vector(dve, job, k, src):
            at = 1 if k is None else 12
            pooling = [] if k is None else [(1, lambda: pool_norm_vector(dve, k, P, src)), (10, lambda: pool_vector(dve, k, src))]

            def split(i):
                return lambda: split_vector(dve, job, P, i)
            return halves(pooling + [(at, lambda: norm_vector(dve, job, P, src, 0 if k is None else 1))] +
                          [(at + 2 + i, split(i)) for i in range(SPLIT + 1)])

        block = ctx.enter_context(nc.Block())

        @block.sync
        def _(sp_):
            mixer_sync(sp_)
            wq_sync(sp_, 0, 0, WQ_EARLY)
            wq_sync(sp_, 0, WQ_EARLY, KD)
            keys_sync(sp_, 0, 0)
            keys_sync(sp_, 0, 1)
            save_parts(sp_, 0, 0, META)
            odd_weights_sync(sp_)
            save_parts(sp_, 1, 1, P)
            for u in range(4):
                fetch_parts(sp_, u, u % 2)
            save_parts(sp_, 2, 1 + TILE_CHUNKS, P)
            meta_prev_sync(sp_)

            def chunk_of(j, s):
                return TILE_CHUNKS * j + 3 + 2 * s

            def pair(j, s):
                fetch_parts(sp_, chunk_of(j, s) + 1, 0)
                fetch_parts(sp_, chunk_of(j, s) + 2, 1)

            def save(j):
                save_parts(sp_, j + 3, TILE_CHUNKS * (j + 2) + 1, P)

            with sp_.Fori(0, 2) as j:
                with sp_.Fori(0, PAIRS) as s:
                    pair(j, s)
                save(j)
            with sp_.Fori(0, 2) as s:
                pair(2, s)
            keys_sync(sp_, 1, 0)
            wq_sync(sp_, 1, 0, 2)
            fetch_parts(sp_, chunk_of(2, 2) + 1, 0)
            wq_sync(sp_, 1, 2, 5)
            fetch_parts(sp_, chunk_of(2, 2) + 2, 1)
            keys_sync(sp_, 1, 1)
            wq_sync(sp_, 1, 5, KD)
            fetch_parts(sp_, chunk_of(2, 3) + 1, 0)
            fetch_parts(sp_, chunk_of(2, 3) + 2, 1)
            save(2)
            with sp_.Fori(3, 6) as j:
                with sp_.Fori(0, PAIRS) as s:
                    pair(j, s)
                save(j)
            with sp_.Fori(0, PAIRS) as s:
                pair(LAST - 1, s)
            with sp_.Fori(0, PAIRS - 2) as s:
                pair(LAST, s)
            fetch_parts(sp_, CHUNKS - 1, 0)
            sp_.wait_ge(s_yadd, 2 + LAST)
            sp_.dma_start(out[0].rearrange("(t p) d -> p t d", p=P), hres[:, 0:XT, :]).then_inc(s_out, 16)
            sp_.wait_ge(s_out, 16)

        @block.gpsimd
        def _(pool):
            n = mixer_constants(pool)
            assert n == MIXER_CONSTANTS
            expert_constants(pool)
            pool.wait_ge(s_proj, 2 * TILES)
            gather_pool(pool, 0, None, 0)
            gather_pool(pool, 1, None, 1)
            gather_pool(pool, 2, 0, 0)

            def pair(j, s):
                u = TILE_CHUNKS * j + 3 + 2 * s
                gather_pool(pool, u, u - 2, 1)
                gather_pool(pool, u + 1, u - 1, 0)

            with pool.Fori(0, LAST) as j:
                with pool.Fori(0, PAIRS) as s:
                    pair(j, s)
            with pool.Fori(0, PAIRS - 1) as s:
                pair(LAST, s)
            gather_pool(pool, None, CHUNKS - 2, 1)
            gather_pool(pool, None, CHUNKS - 1, 0)

        @block.scalar
        def _(act):
            mixer_scalar(act)
            act.wait_ge(s_mix, 2)
            norm_scalar(act, 0, META, META_ROWS)
            keys_scalar(act, 0, 0)
            keys_scalar(act, 0, 1)
            transposed_scalar(act, 0, META)
            act.wait_ge(s_mix, 4)
            norm_scalar(act, 1, P, tile_of(0))
            meta_scalar(act)
            transposed_scalar(act, 1, P)
            query_scalar(act, 1, P, QUERY_BANK)
            queryT_scalar(act, 1, P)
            tail_scalar(act, 0, P, 2)
            query_scalar(act, 2, P, QUERY_BANK)
            meta_tables_scalar(act)
            queryT_scalar(act, 2, P)
            with act.Fori(2, PAIRS) as s:
                query_scalar(act, first_piece(1) + s, P, QUERY_BANK)
                queryT_scalar(act, first_piece(1) + s, P)
            tail_scalar(act, 1, P)

            def expand(v, par, pos, hooks=(), tables=None, stage=True, v_next=True):
                def stages():
                    if tables is not None:
                        act.wait_ge(s_idx, tables)
                    if stage:
                        stage_u(act, v + 3, 1 - par)
                    if v_next:
                        stage_v(act, v + 1, 1 - par)
                own = [(1, lambda: gelu_scalar(act, v + 1)), (8, stages)] if v_next else []
                columns_scalar(act, v, par, pos, own + list(hooks))

            def pair(j, s, first=(), second=(), tables=None, stage_last=True):
                v = TILE_CHUNKS * j + 1 + 2 * s
                expand(v, 1, 2 * CHUNK * s, first, tables)
                expand(v + 1, 0, 2 * CHUNK * s + CHUNK, second, stage=stage_last)

            def iteration(j, start=(), keys=()):
                with act.Fori(0, 2) as s:
                    pair(j, s, *routing_scalar(act, j + 2, s))
                pair(j, 2, [(1, lambda: tail_scalar(act, j + 2, P))], keys, tables=j + 3)
                pair(j, 3, *start)

            act.wait_ge(s_idx, 2)
            stage_u(act, 0, 0)
            stage_u(act, 1, 1)
            act.wait_ge(s_mix, 2 * TILES)
            norm_scalar(act, 2, P, tile_of(1))
            stage_u(act, 2, 0)
            stage_v(act, 0, 0)
            gelu_scalar(act, 0)
            transposed_scalar(act, 2, P)
            act.wait_ge(s_setup, SETUP_STEPS)
            expand(0, 0, 0)
            pool_norm_scalar(act, 0, 3, META, META_ROWS)

            with act.Fori(0, 2) as j:
                iteration(j, start_stages_scalar(act, j + 3, None, tile_of(j + 2)))
            iteration(2, start_stages_scalar(act, 5, 1, tile_of(0)),
                      [(4, lambda: keys_scalar(act, 1, 0)), (11, lambda: keys_scalar(act, 1, 1))])
            with act.Fori(3, 6) as j:
                iteration(j, start_stages_scalar(act, j + 3, j - 1, tile_of(j - 2)))
            iteration(LAST - 1)
            with act.Fori(0, PAIRS - 2) as s:
                pair(LAST, s)
            pair(LAST, PAIRS - 2, stage_last=False)
            expand(CHUNKS - 2, 1, 2 * CHUNK * (PAIRS - 1), stage=False)
            expand(CHUNKS - 1, 0, 2 * CHUNK * (PAIRS - 1) + CHUNK, v_next=False)

        @block.vector
        def _(dve):
            mixer_vector(dve)
            dve.wait_ge(s_iota, 1)
            nc.vector.memset(tv[:, :, :], 0.0).then_inc(s_routed, 1)
            dve.wait_ge(s_routed, 1)

            nc.vector.memset(cand[:, :], 0.0).then_inc(s_cleared, 1)
            norm_vector(dve, 0, META, META_ROWS, 0)
            add_projected(dve, 2)
            add_projected(dve, 3)
            for i in range(SPLIT + 1):
                split_vector(dve, 0, META, i)
            norm_vector(dve, 1, P, tile_of(0), 0)
            for stage in topk_stages(dve, 0, 0, P, meta=True):
                stage()
            logits_vector(dve, 0, P, 2)
            for i in range(SPLIT + 1):
                split_vector(dve, 1, P, i)
            gates_vector(dve, 0, P, 2)
            for s in range(PAIRS):
                stages = topk_stages(dve, first_piece(1) + s, s, P)
                for stage in stages[:-1]:
                    stage()
                if s == 0:
                    dve.wait_ge(s_gateT, 1)
                stages[-1]()
                if s + 1 < PAIRS:
                    add_projected(dve, 4 + s)
                if s == 0:
                    meta_tables_vector(dve)
            logits_vector(dve, 1, P)
            gates_vector(dve, 1, P)
            tables_vector(dve, 1, P, META, 0)
            for i in range(3 + PAIRS, 2 * TILES):
                add_projected(dve, i)

            def pair(j, s, first=(), second=()):
                u = TILE_CHUNKS * j + 3 + 2 * s
                dots_vector(dve, u, 1, first)
                dots_vector(dve, u + 1, 0, second)

            def iteration(j, layer, start=()):
                job = j + 2
                with dve.Fori(0, 2) as s:
                    pair(j, s, *routing_vector(dve, job, s))
                pair(j, 2, [(0, lambda: logits_vector(dve, job, P)), (2, lambda: gates_vector(dve, job, P)),
                            (4, lambda: tables_vector(dve, job, P, META + P * (j + 1), layer))])
                pair(j, 3, *start)
                take_sum(dve, j + 1, tile_of(j % XT), P)

            dots_vector(dve, 0, 0, first=True)
            dots_vector(dve, 1, 1, [(4, lambda: norm_vector(dve, 2, P, tile_of(1), 0))] +
                        [(6 + i, lambda i=i: split_vector(dve, 2, P, i)) for i in range(SPLIT + 1)])
            dots_vector(dve, 2, 0)
            take_sum(dve, 0, META_ROWS, META)
            pool_norm_vector(dve, 0, META, META_ROWS)

            with dve.Fori(0, 2) as j:
                iteration(j, 0, start_stages_vector(dve, j + 3, None, tile_of(j + 2)))
            iteration(2, 0, start_stages_vector(dve, 5, 1, tile_of(0)))
            with dve.Fori(3, 6) as j:
                iteration(j, 1, start_stages_vector(dve, j + 3, j - 1, tile_of(j - 2)))
            iteration(LAST - 1, 1)
            with dve.Fori(0, PAIRS - 1) as s:
                pair(LAST, s)
            gelu_weights(dve, CHUNKS - 1, 0)
            take_sum(dve, LAST + 1, tile_of(XT - 1), P)

        @block.tensor
        def _(pe):
            mixer_tensor(pe)
            keys_tensor(pe, 0, 0)
            keys_tensor(pe, 0, 1)

            project_tensor(pe, 2)
            project_tensor(pe, 3)
            start_tensor(pe, 0, META, 0)
            meta_queries_tensor(pe)
            meta_scores_tensor(pe)
            start_tensor(pe, 1, P, 0)
            pe.wait_ge(s_hbT, 4)
            query_tensor(pe, first_piece(1), 0, P, 0, KD, QUERY_BANK)

            def piece(s, more=True):
                queryT_tensor(pe, first_piece(1) + s, P)
                pe.wait_ge(s_read, first_piece(1) + s)
                scores_tensor(pe, first_piece(1) + s, s, P)
                if more:
                    query_tensor(pe, first_piece(1) + s + 1, s + 1, P, 0, KD, QUERY_BANK)
            for s in range(PAIRS):
                piece(s, more=s + 1 < PAIRS)
                project_tensor(pe, 4 + s)
                if s == 0:
                    meta_tail_tensor(pe)
            for i in range(4 + PAIRS, 2 * TILES):
                project_tensor(pe, i)
            tail_tensor(pe, 1, P)

            def pair(j, s, first=(), second=()):
                u = TILE_CHUNKS * j + 3 + 2 * s
                fetched = PAIRS * j + 1 + s
                experts_tensor(pe, u, u - 2, 1, fetched + 1, first)
                experts_tensor(pe, u + 1, u - 1, 0, fetched + 2, second)

            def iteration(j, start=(), keys=()):
                open_sum(pe, j + 1)
                with pe.Fori(0, 2) as s:
                    pair(j, s, *routing_tensor(pe, j + 2, s))
                pair(j, 2, [(3, lambda: tail_tensor(pe, j + 2, P))], keys)
                pair(j, 3, *start)
                close_sum(pe)

            pe.wait_ge(s_setup, SETUP_STEPS)
            pe.wait_ge(s_mix, 2 * TILES)
            experts_tensor(pe, 0, None, 0, 1)
            experts_tensor(pe, 1, None, 1, 1, [(5, lambda: start_tensor(pe, 2, P, 0))])
            open_sum(pe, 0)
            experts_tensor(pe, 2, 0, 0, 2)
            close_sum(pe)
            with pe.Fori(0, 2) as j:
                iteration(j, start_stages_tensor(pe, j + 3, None))
            iteration(2, start_stages_tensor(pe, 5, 1),
                      [(2, lambda: keys_tensor(pe, 1, 0)), (9, lambda: keys_tensor(pe, 1, 1))])
            with pe.Fori(3, 6) as j:
                iteration(j, start_stages_tensor(pe, j + 3, j - 1))
            iteration(LAST - 1)
            open_sum(pe, LAST + 1)
            with pe.Fori(0, PAIRS - 1) as s:
                pair(LAST, s)
            experts_tensor(pe, None, CHUNKS - 2, 1, 0)
            experts_tensor(pe, None, CHUNKS - 1, 0, 0)
            close_sum(pe)


_INS = ["x", "meta_tokens", "even_norm_g", "even_w_in", "even_q_norm_g", "even_k_norm_g", "even_conv_w", "even_w_out",
        "odd_norm_g", "odd_pool_w", "odd_pool_scale", "ffn_norm_g", "peer_w_query", "peer_sub_keys", "peer_u", "peer_v"]


def kernel(**inputs):
    import concourse.bacc as bacc
    from concourse.bass_utils import run_bass_kernel_spmd

    nc = bacc.Bacc("TRN2", target_bir_lowering=False, num_devices=1)
    arrays, args = {}, []
    for name in _INS:
        a = np.ascontiguousarray(inputs[name])
        arrays[f"in_{name}"] = a
        args.append(nc.dram_tensor(f"in_{name}", a.shape, mybir.dt.from_np(a.dtype), kind="ExternalInput").ap())
    out = nc.dram_tensor("out", (1, SEQ, D), F32, kind="ExternalOutput").ap()
    program(nc, *args, out)
    r = run_bass_kernel_spmd(nc, [arrays], core_ids=[0])
    return r.results[0]["out"]
```
